# Optimizing a Trainium2 kernel written in Bass

```python
import math
import jax, jax.numpy as jnp
from jax import lax
import numpy as np

D_MODEL = 1024
BATCH = 1
SEQ = 256
DEPTH = 1

RMS_EPS = 1e-5
ATTN_HEADS = 16
ATTN_KV_HEADS = 2
HEAD_DIM = 64
WINDOW = 128
Q_DIM = ATTN_HEADS * HEAD_DIM
KV_DIM = ATTN_KV_HEADS * HEAD_DIM
SSM_EXPAND = 2
D_INNER = SSM_EXPAND * D_MODEL
SSM_HEAD_DIM = 64
SSM_HEADS = D_INNER // SSM_HEAD_DIM
SSM_GROUPS = 4
D_STATE = 128
CONV_WIDTH = 4
CHUNK = 128
XBC_DIM = D_INNER + 2 * SSM_GROUPS * D_STATE
IN_COLS = Q_DIM + 2 * KV_DIM + D_INNER + XBC_DIM + SSM_HEADS
IN_SPLITS = (Q_DIM, Q_DIM + KV_DIM, Q_DIM + 2 * KV_DIM, Q_DIM + 2 * KV_DIM + D_INNER, Q_DIM + 2 * KV_DIM + D_INNER + XBC_DIM)
N_BRANCHES = 2
MEM_TOKENS = 256
CROSS_HEADS = 4
CROSS_HEAD_DIM = D_MODEL // CROSS_HEADS
N_EXPERTS = 32
TOP_K = 4
D_EXPERT = D_MODEL
SWIGLU_LIMIT = 7.0
SWIGLU_ALPHA = 1.702

kernel_name = "hybrid_swa_ssd_moe_block"

def rmsnorm(x, w):
    xf = x.astype(jnp.float32)
    y = xf * lax.rsqrt(jnp.mean(xf * xf, axis=-1, keepdims=True) + RMS_EPS)
    return (y * w.astype(jnp.float32)).astype(x.dtype)

def alibi_slopes(n_heads):
    return jnp.exp2(-8.0 * jnp.arange(1, n_heads + 1, dtype=jnp.float32) / n_heads)

def sliding_window_attention(q, k, v, sinks):
    bsz, seq, _ = q.shape
    nb = seq // WINDOW
    grp = ATTN_HEADS // ATTN_KV_HEADS
    qb = q.reshape(bsz, nb, WINDOW, ATTN_KV_HEADS, grp, HEAD_DIM)
    kb = k.reshape(bsz, nb, WINDOW, ATTN_KV_HEADS, HEAD_DIM)
    vb = v.reshape(bsz, nb, WINDOW, ATTN_KV_HEADS, HEAD_DIM)

    def with_prev(t):
        prev = jnp.concatenate([jnp.zeros_like(t[:, :1]), t[:, :-1]], axis=1)
        return jnp.concatenate([prev, t], axis=2)

    kk, vv = with_prev(kb), with_prev(vb)
    scores = jnp.einsum('bnqkgd,bnskd->bnkgqs', qb, kk).astype(jnp.float32) * (HEAD_DIM ** -0.5)
    qi = jnp.arange(WINDOW)[:, None]
    kj = jnp.arange(2 * WINDOW)[None, :]
    dist = qi + WINDOW - kj
    in_window = (dist >= 0) & (dist < WINDOW)
    has_prev = (jnp.arange(nb)[:, None, None] > 0) | (kj >= WINDOW)[None]
    mask = in_window[None] & has_prev
    slopes = alibi_slopes(ATTN_HEADS).reshape(ATTN_KV_HEADS, grp)
    bias = -slopes[:, :, None, None] * dist.astype(jnp.float32)[None, None]
    scores = jnp.where(mask[None, :, None, None], scores + bias, -jnp.inf)
    sink = sinks.astype(jnp.float32).reshape(ATTN_KV_HEADS, grp)[:, :, None, None]
    m = jnp.maximum(jnp.max(scores, axis=-1, keepdims=True), sink)
    p = jnp.exp(scores - m)
    probs = p / (jnp.sum(p, axis=-1, keepdims=True) + jnp.exp(sink - m))
    out = jnp.einsum('bnkgqs,bnskd->bnqkgd', probs.astype(v.dtype), vv)
    return out.reshape(bsz, seq, Q_DIM)

def causal_dwconv(u, w):
    ch = u.shape[-1]
    return lax.conv_general_dilated(u, w[:, None, :].astype(u.dtype), window_strides=(1,),
                                    padding=[(CONV_WIDTH - 1, 0)],
                                    dimension_numbers=('NWC', 'WIO', 'NWC'),
                                    feature_group_count=ch)

def ssd_chunked(xs, dt, a_heads, bm, cm):
    b, seq = xs.shape[0], xs.shape[1]
    nc = seq // CHUNK
    rep = SSM_HEADS // SSM_GROUPS
    x = xs.astype(jnp.float32).reshape(b, nc, CHUNK, SSM_GROUPS, rep, SSM_HEAD_DIM)
    dtc = dt.reshape(b, nc, CHUNK, SSM_GROUPS, rep)
    bc = bm.astype(jnp.float32).reshape(b, nc, CHUNK, SSM_GROUPS, D_STATE)
    cc = cm.astype(jnp.float32).reshape(b, nc, CHUNK, SSM_GROUPS, D_STATE)
    a = jnp.transpose(dtc * a_heads.reshape(SSM_GROUPS, rep), (0, 3, 4, 1, 2))
    a_cum = jnp.cumsum(a, axis=-1)
    xdt = x * dtc[..., None]
    causal = jnp.tril(jnp.ones((CHUNK, CHUNK), dtype=bool))
    seg = a_cum[..., :, None] - a_cum[..., None, :]
    lmat = jnp.exp(jnp.where(causal, seg, -jnp.inf))
    cb = jnp.einsum('bclgn,bcsgn->bgcls', cc, bc)
    y_diag = jnp.einsum('bgcls,bgrcls,bcsgrp->bclgrp', cb, lmat, xdt)
    decay_states = jnp.exp(a_cum[..., -1:] - a_cum)
    states = jnp.einsum('bclgn,bgrcl,bclgrp->cbgrpn', bc, decay_states, xdt)
    chunk_decay = jnp.moveaxis(jnp.exp(a_cum[..., -1]), -1, 0)

    def step(carry, inp):
        st, dec = inp
        return carry * dec[..., None, None] + st, carry

    _, prev = lax.scan(step, jnp.zeros(states.shape[1:], jnp.float32), (states, chunk_decay))
    y_off = jnp.einsum('bclgn,cbgrpn,bgrcl->bclgrp', cc, prev, jnp.exp(a_cum))
    y = (y_diag + y_off).reshape(b, seq, SSM_HEADS, SSM_HEAD_DIM)
    return y.astype(xs.dtype)

def mamba2_mixer(z, xbc, dt_raw, conv_w, conv_b, dt_bias, a_log, d_skip, norm_w):
    bsz, seq, _ = z.shape
    xbc = jax.nn.silu(causal_dwconv(xbc, conv_w) + conv_b)
    xs, bm, cm = jnp.split(xbc, [D_INNER, D_INNER + SSM_GROUPS * D_STATE], axis=-1)
    xs = xs.reshape(bsz, seq, SSM_HEADS, SSM_HEAD_DIM)
    bm = bm.reshape(bsz, seq, SSM_GROUPS, D_STATE)
    cm = cm.reshape(bsz, seq, SSM_GROUPS, D_STATE)
    dt = jax.nn.softplus(dt_raw.astype(jnp.float32) + dt_bias.astype(jnp.float32))
    a_heads = -jnp.exp(a_log.astype(jnp.float32))
    y = ssd_chunked(xs, dt, a_heads, bm, cm) + xs * d_skip[:, None]
    y = y.reshape(bsz, seq, D_INNER) * jax.nn.silu(z)
    yf = y.astype(jnp.float32).reshape(bsz, seq, SSM_GROUPS, D_INNER // SSM_GROUPS)
    yf = yf * lax.rsqrt(jnp.mean(yf * yf, axis=-1, keepdims=True) + RMS_EPS)
    return (yf.reshape(bsz, seq, D_INNER) * norm_w.astype(jnp.float32)).astype(z.dtype)

def cross_attention(hn, mn, w_cq, w_ckv, w_co):
    bsz, seq, _ = hn.shape
    q = (hn @ w_cq).reshape(bsz, seq, CROSS_HEADS, CROSS_HEAD_DIM)
    k, v = jnp.split(mn @ w_ckv, 2, axis=-1)
    k = k.reshape(bsz, -1, CROSS_HEADS, CROSS_HEAD_DIM)
    v = v.reshape(bsz, -1, CROSS_HEADS, CROSS_HEAD_DIM)
    s = jnp.einsum('bthd,bmhd->bhtm', q, k).astype(jnp.float32) * (CROSS_HEAD_DIM ** -0.5)
    p = jax.nn.softmax(s, axis=-1)
    o = jnp.einsum('bhtm,bmhd->bthd', p.astype(v.dtype), v).reshape(bsz, seq, D_MODEL)
    return o @ w_co

def moe_ffn(u, w_router, b_router, w_gu, b_gu, w_dn, b_dn):
    bsz, seq, _ = u.shape
    t = u.reshape(-1, D_MODEL)
    logits = (t @ w_router + b_router).astype(jnp.float32)
    top_v, top_i = lax.top_k(logits, TOP_K)
    top_w = jax.nn.softmax(top_v, axis=-1)
    gate = jnp.sum(jax.nn.one_hot(top_i, N_EXPERTS, dtype=jnp.float32) * top_w[..., None], axis=1)
    gate = gate.astype(t.dtype)
    y = jnp.zeros_like(t)
    for e in range(N_EXPERTS):
        gu = t @ w_gu[e] + b_gu[e]
        g, up = jnp.split(gu, 2, axis=-1)
        g = jnp.minimum(g, SWIGLU_LIMIT)
        up = jnp.clip(up, -SWIGLU_LIMIT, SWIGLU_LIMIT)
        act = (up + 1.0) * (g * jax.nn.sigmoid(SWIGLU_ALPHA * g))
        y = y + gate[:, e:e + 1] * (act @ w_dn[e] + b_dn[e])
    return y.reshape(bsz, seq, D_MODEL)

def setup_inputs(seed: int = 0) -> dict:
    key = jax.random.key(seed)
    ks = iter(jax.random.split(key, 40))
    f32 = jnp.float32
    L = DEPTH

    def dense(shape, fan_in):
        return jax.random.normal(next(ks), shape, f32) * (fan_in ** -0.5)

    def gain(shape):
        return 1.0 + 0.02 * jax.random.normal(next(ks), shape, f32)

    def small(shape, scale=0.01):
        return scale * jax.random.normal(next(ks), shape, f32)

    x = jax.random.normal(next(ks), (BATCH, SEQ, D_MODEL), f32)
    mem = jax.random.normal(next(ks), (BATCH, MEM_TOKENS, D_MODEL), f32)
    dt0 = jnp.exp(jax.random.uniform(next(ks), (L, SSM_HEADS), f32, math.log(1e-3), math.log(1e-1)))
    dt_bias = dt0 + jnp.log(-jnp.expm1(-dt0))
    a_log = jnp.log(jax.random.uniform(next(ks), (L, SSM_HEADS), f32, 1.0, 16.0))
    return {
        "x": x,
        "mem": mem,
        "norm_mix_w": gain((L, D_MODEL)),
        "w_in": dense((L, D_MODEL, IN_COLS), D_MODEL),
        "w_gate": dense((L, D_MODEL, N_BRANCHES * D_MODEL), D_MODEL),
        "b_gate": small((L, N_BRANCHES * D_MODEL), 0.1),
        "attn_sinks": small((L, ATTN_HEADS), 0.5),
        "conv_w": dense((L, CONV_WIDTH, XBC_DIM), CONV_WIDTH),
        "conv_b": small((L, XBC_DIM), 0.02),
        "dt_bias": dt_bias,
        "a_log": a_log,
        "d_skip": gain((L, SSM_HEADS)),
        "ssm_norm_w": gain((L, D_INNER)),
        "w_attn_o": dense((L, Q_DIM, D_MODEL), Q_DIM),
        "w_ssm_o": dense((L, D_INNER, D_MODEL), D_INNER),
        "w_out": dense((L, D_MODEL, D_MODEL), D_MODEL),
        "norm_cross_w": gain((L, D_MODEL)),
        "norm_mem_w": gain((L, D_MODEL)),
        "w_cq": dense((L, D_MODEL, D_MODEL), D_MODEL),
        "w_ckv": dense((L, D_MODEL, 2 * D_MODEL), D_MODEL),
        "w_co": dense((L, D_MODEL, D_MODEL), D_MODEL),
        "norm_ffn_w": gain((L, D_MODEL)),
        "w_router": dense((L, D_MODEL, N_EXPERTS), D_MODEL),
        "b_router": small((L, N_EXPERTS), 0.01),
        "w_gu": dense((L, N_EXPERTS, D_MODEL, 2 * D_EXPERT), D_MODEL),
        "b_gu": small((L, N_EXPERTS, 2 * D_EXPERT), 0.01),
        "w_dn": dense((L, N_EXPERTS, D_EXPERT, D_MODEL), D_EXPERT),
        "b_dn": small((L, N_EXPERTS, D_MODEL), 0.01),
        "final_norm_w": gain((D_MODEL,)),
    }

def reference(x, mem, norm_mix_w, w_in, w_gate, b_gate, attn_sinks, conv_w, conv_b, dt_bias, a_log, d_skip,
              ssm_norm_w, w_attn_o, w_ssm_o, w_out, norm_cross_w, norm_mem_w, w_cq, w_ckv, w_co,
              norm_ffn_w, w_router, b_router, w_gu, b_gu, w_dn, b_dn, final_norm_w):
    bsz, seq, _ = x.shape
    h = x
    for l in range(DEPTH):
        u = rmsnorm(h, norm_mix_w[l])
        q, k, v, z, xbc, dt_raw = jnp.split(u @ w_in[l], IN_SPLITS, axis=-1)
        attn = sliding_window_attention(q, k, v, attn_sinks[l])
        ssm = mamba2_mixer(z, xbc, dt_raw, conv_w[l], conv_b[l], dt_bias[l], a_log[l], d_skip[l], ssm_norm_w[l])
        gates = jax.nn.sigmoid(u @ w_gate[l] + b_gate[l]).reshape(bsz, seq, N_BRANCHES, D_MODEL)
        merged = gates[..., 0, :] * (attn @ w_attn_o[l]) + gates[..., 1, :] * (ssm @ w_ssm_o[l])
        h = h + merged @ w_out[l]
        h = h + cross_attention(rmsnorm(h, norm_cross_w[l]), rmsnorm(mem, norm_mem_w[l]), w_cq[l], w_ckv[l], w_co[l])
        h = h + moe_ffn(rmsnorm(h, norm_ffn_w[l]), w_router[l], b_router[l], w_gu[l], b_gu[l], w_dn[l], b_dn[l])
    return rmsnorm(h, final_norm_w)


_drawn_inputs = setup_inputs


def setup_inputs(seed=0):
    import zlib

    import numpy as np

    out = dict(_drawn_inputs(seed))
    spreads = {}
    factors = {'d_skip': 3.332,
     'norm_cross_w': 8.0,
     'norm_mem_w': 8.0,
     'b_router': 23.309,
     'b_gu': 64.0,
     'b_dn': 64.0,
     'final_norm_w': 7.535,
     'norm_ffn_w': 8.0}
    for name, (base, spread) in spreads.items():
        noise = np.random.default_rng([zlib.crc32(name.encode()), seed]).standard_normal(out[name].shape)
        drawn = base * np.exp(spread * noise) if base else spread * noise
        out[name] = __import__('jax').numpy.asarray(drawn.astype(out[name].dtype))
    for name, factor in factors.items():
        out[name] = (out[name] * factor).astype(out[name].dtype)
    return out
```

```python
from contextlib import ExitStack

import concourse.bass as bass
import numpy as np
from concourse import mybir

P = 128
F32 = mybir.dt.float32
F32R = mybir.dt.float32r
BF16 = mybir.dt.bfloat16
I32 = mybir.dt.int32
U32 = mybir.dt.uint32
ALU = mybir.AluOpType
ACT = mybir.ActivationFunctionType
AX = mybir.AxisListType.X

D = 1024
T = 256
NT = T // P
KD = D // P
HQ, HKV, HD = 16, 2, 64
QD, KVD = HQ * HD, HKV * HD
DI = 2 * D
SH = DI // 64
SG = 4
NS = 128
GH = SH // SG
XBC = DI + 2 * SG * NS
C_K, C_V, C_Z, C_X = QD, QD + KVD, QD + 2 * KVD, QD + 2 * KVD + DI
C_B, C_C, C_DT = C_X + DI, C_X + DI + SG * NS, C_X + XBC
CH, CHD = 4, 256
NE, TOPK = 32, 4
EPS = 1e-5
LIMIT, ALPHA = 7.0, 1.702
SLOTS = 64
ROUNDS = T // SLOTS
MASKED = -1.0e30

TK, TN = 4, 512
RAW, RAW_MOE = 4, 8
HL, HL_MOE = 2, 4
DIRECT = (("D0", 1), ("D1", 1))
BY_POOL = (("U1", 0), ("U0", 1))

V_MIX, V_CROSS, V_MEM = 0, KD, 2 * KD
V_CONVW = 3 * KD
V_CONVB = V_CONVW + 4 * (XBC // P)
V_SSMW = V_CONVB + XBC // P
V_SKIP = V_SSMW + DI // P
NV = V_SKIP + DI // P
R_DTB, R_ALOG, R_SINK, R_BR = 0, SH, 2 * SH, 2 * SH + HQ
NR = R_BR + NE


def dense_blocks():
    x = lambda g: [("x", g, "w_in", 0, C_X + TN * g, 2), ("z", g, "w_in", 0, C_Z + TN * g, 2)]
    so = lambda g: [("so", (g, n), "w_ssm_o", TN * g, TN * n, 1) for n in range(2)]
    gate = lambda b: [("gate", (b, n), "w_gate", 0, D * b + TN * n, 2) for n in range(2)]
    out = [("kvdt", 0, "w_in", 0, C_K, 2), ("q", 0, "w_in", 0, 0, 2), ("q", 1, "w_in", 0, TN, 2),
           ("B", 0, "w_in", 0, C_B, 2), ("C", 0, "w_in", 0, C_C, 2)]
    out += x(0) + x(1) + x(2) + so(0) + [x(3)[0]] + so(1) + [x(3)[1]] + so(2)
    out += [("ao", n, "w_attn_o", 0, TN * n, 2) for n in range(2)]
    out += gate(0) + so(3) + gate(1)
    out += [("ck", n, "w_ckv", 0, TN * n, 2) for n in range(2)]
    out += [("cv", n, "w_ckv", 0, D + TN * n, 2) for n in range(2)]
    out += [("o", n, "w_out", 0, TN * n, 2) for n in range(2)]
    out += [("cq", n, "w_cq", 0, TN * n, 2) for n in range(2)]
    out += [("co", n, "w_co", 0, TN * n, 2) for n in range(2)]
    return out


BLOCKS = dense_blocks()
LAST_TILE = {}
_t = 0
for _b in BLOCKS:
    _t += _b[5]
    LAST_TILE[_b[:2]] = _t - 1
TD = _t


def dense_stages():
    at = {}

    def put(tile, *stage):
        at.setdefault(tile, []).append(stage)

    put(3, "decay", 0)
    q0 = LAST_TILE["q", 0]
    for hp in range(HQ // 2):
        put(q0 + hp + 4, "pv", hp)
        put(q0 + hp + 3, "pt", hp)
        put(q0 + hp + 2, "probs", hp)
        put(q0 + hp + 1, "scores", hp)
    put(LAST_TILE["C", 0] + 2, "cb", 0)
    for g in range(SG):
        z = LAST_TILE["z", g]
        put(z + 1, "xt", g)
        put(z + 2, "state", g)
        for q in range(4):
            put(z + 1 + q, "decays", g, q)
            put(z + 2 + q, "y", g, q)
        put(z + 6, "norm", g)
    put(LAST_TILE["gate", (1, 1)], "merged", 0)
    put(LAST_TILE["gate", (1, 1)], "mem", 0)
    put(LAST_TILE["o", 1], "cross_in", 0)
    put(LAST_TILE["cq", 1], "cross", 0)
    put(LAST_TILE["co", 1], "router", 0)
    return at


STAGES = dense_stages()
ORDER = ["decay", "pv", "pt", "probs", "scores", "cb", "norm", "y", "xt", "state", "decays",
         "merged", "mem", "cross_in", "cross", "router"]


def stages_after(tile):
    return sorted(STAGES.get(tile, []), key=lambda s: ORDER.index(s[0]))


def body_blocks(last):
    out = []
    for a in range(2):
        out += [("G1", a), ("U1", a)]
        if not (last and a == 1):
            out += [("G0", a + 1), ("U0", a + 1)]
        out += [("D0", a), ("D1", a)]
    return out


class Pass:

    def __init__(self, last):
        self.blocks = body_blocks(last)
        self.tiles = [(kind, a, half) for kind, a in self.blocks for half in range(2)]
        self.is_split = [(kind, half) not in DIRECT for kind, _, half in self.tiles]
        self.splits = [j for j, split in enumerate(self.is_split) if split]

        self.by_pool = [(kind, half) in BY_POOL for kind, _, half in self.tiles]

    def splits_before(self, j):
        return sum(self.is_split[:j])

    def pool_before(self, j):
        return sum(self.by_pool[:j])


EVERY, LAST = Pass(False), Pass(True)
NB, NTILE, NSPLIT = len(EVERY.blocks), len(EVERY.tiles), len(EVERY.splits)
NDIRECT, NPOOL = NTILE - NSPLIT, sum(EVERY.by_pool)
PRO = 4
assert NSPLIT % HL_MOE == 0 and NTILE % RAW_MOE == 0


def layer(nc, A, out):
    ctx = ExitStack()
    with ctx:
        top = [-(-nc.sbuf_base // 32) * 32]

        def place(name, shape, dt=F32, at=None):
            size = int(np.prod(shape[1:])) * (2 if dt == BF16 else 4)
            where = top[0] if at is None else at
            t = nc.alloc_sbuf_tensor_at(name, shape, dt, offset=where)
            if at is None:
                top[0] += -(-size // 32) * 32
            return t

        KB = 1024
        raw = [place(f"raw{i}", [P, TK, TN]) for i in range(RAW)]
        w_hi = [place(f"w_hi{i}", [P, TK, TN], F32R) for i in range(HL)]
        w_lo = [place(f"w_lo{i}", [P, TK, TN], F32R) for i in range(HL)]
        h = place("h", [P, NT, D])
        ident = place("ident", [P, P])
        upto = place("upto", [P, P])
        before = place("before", [P, P])
        ones = place("ones", [P, P])
        iota = place("iota", [P, SLOTS])
        pick = place("pick", [P, ROUNDS * NE])
        vecs = place("vecs", [P, NV])
        rows = place("rows", [P, NR])
        stat = place("stat", [P, 64])
        dts = place("dts", [P, NT, SH])
        a_t = place("a_t", [P, NT, SH])
        acum = place("acum", [P, NT, SH])
        ddt = place("ddt", [P, SH])
        tmp32 = place("tmp32", [P, 6, NT * SH])
        cur_small = place("cur_small", [P, 1])
        w_r = place("w_r", [P, KD, NE])
        arena = top[0]

        def overlay(start):
            cursor = [arena + start]

            def put(name, shape, dt=F32):
                t = place(name, shape, dt, at=cursor[0])
                cursor[0] += -(-int(np.prod(shape[1:])) * (2 if dt == BF16 else 4) // 32) * 32
                assert cursor[0] <= nc.sbuf_usable_end, (name, cursor[0])
                return t
            return put, cursor

        put, cur = overlay(0)
        xta = put("xta", [P, 2, KD, T], F32R)
        xtb = put("xtb", [P, 2, KD, T], F32R)
        xts = put("xts", [P, 2, TK, T], F32R)
        ssm = put("ssm", [P, NT, D])
        att = put("att", [P, NT, D])
        ssd0 = cur[0] - arena
        zt = [put(f"zt{i}", [P, TK, T]) for i in range(2)]
        xt = [put(f"xt{i}", [P, TK, T]) for i in range(2)]
        bt = put("bt", [P, TK, T])
        ct = put("ct", [P, TK, T])
        conv = put("conv", [P, TK, T])
        cbt = put("cbt", [P, NT, SG, P])
        btok = put("btok", [P, SG, NS])
        v2 = put("v2", [P, NT, HKV, P])
        kpad = put("kpad", [P, HKV, 2, T])
        at0 = cur[0] - arena
        qt = put("qt", [P, KD, T])
        dist = put("dist", [P, 2 * P])
        sc = [put(f"sc{i}", [P, 2, 3 * P]) for i in range(2)]
        pt = put("pt", [P, 2, 3, P])
        put, cur = overlay(at0)
        xdt = put("xdt", [P, NT, TN])
        xdd = put("xdd", [P, TN])
        h0 = put("h0", [P, TN])
        seg = [put(f"seg{i}", [P, 4, P]) for i in range(2)]
        gm = [put(f"gm{i}", [P, 4, P]) for i in range(2)]
        ea = put("ea", [P, 4, P])
        cte = [put(f"cte{i}", [P, 4, P]) for i in range(2)]
        yt = put("yt", [P, TK, T])
        ysq = put("ysq", [P, TK, T])
        rs = put("rs", [P, T])
        put, cur = overlay(ssd0)
        memx = put("memx", [P, NT, D])
        bgate = put("bgate", [P, 2 * D])
        ckt = put("ckt", [P, KD, T])
        sig = put("sig", [P, NT, TN])
        cv = put("cv", [P, NT, D])
        late = cur[0] - arena
        xtm = put("xtm", [P, 2, KD, T], F32R)
        put, cur = overlay(late)
        cqt = put("cqt", [P, KD, T])
        xs = put("xs", [P, NT, D])
        put, cur = overlay(ssd0)
        csc = [put(f"csc{i}", [P, NT, T]) for i in range(2)]
        cpt = [put(f"cpt{i}", [P, NT, T]) for i in range(2)]
        put, cur = overlay(0)
        raw_moe = raw + [put(f"raw{i}", [P, TK, TN]) for i in range(RAW, RAW_MOE)]
        hi_moe = w_hi + [put(f"w_hi{i}", [P, TK, TN], F32R) for i in range(HL, HL_MOE)]
        lo_moe = w_lo + [put(f"w_lo{i}", [P, TK, TN], F32R) for i in range(HL, HL_MOE)]
        fw = place("fw", [P, D], at=cur[0])
        xp = [put(f"xp{i}", [P, NT, D], BF16) for i in range(3)]
        btab = put("btab", [P, 3 * D], F32R)
        oex = put("oex", [P, D])
        xe = [put(f"xe{i}", [P, KD, P], F32R) for i in range(2)]
        ae = [put(f"ae{i}", [P, KD, P], F32R) for i in range(2)]
        af = put("af", [P, KD, SLOTS])
        back = put("back", [P, T])
        sel = [put(f"sel{i}", [P, NT, SLOTS], BF16) for i in range(2)]
        selg = put("selg", [P, NT, P])
        bsel = [put(f"bsel{i}", [P, P], F32R) for i in range(2)]
        gl = put("gl", [P, TN])
        gg, low = gl[0:SLOTS, :], gl[SLOTS:P, :]
        gs = put("gs", [SLOTS, TN])
        uu = put("uu", [SLOTS, TN])
        aa = put("aa", [P, TN])
        pos4 = put("pos4", [P, NT, ROUNDS * NE])
        gate4 = put("gate4", [P, NT, ROUNDS * NE])
        logit = put("logit", [P, NT, NE])
        mask = put("mask", [P, NT, NE])
        gate = put("gate", [P, NT, NE])
        eq = put("eq", [P, NE])
        top8 = put("top8", [P, NT, 8])
        idx8 = put("idx8", [P, NT, 8], U32)
        idxf = put("idxf", [P, NT, 8])
        last_pass = put("last_pass", [P, 1], I32)
        put, cur = overlay((RAW_MOE - RAW + 1) * 8 * KB)
        bst = put("bst", [P, 3 * D])
        put, cur = overlay((RAW_MOE - RAW + 3) * 8 * KB)
        u2t = put("u2t", [P, KD, T])
        put, cur = overlay(late)
        wbc = put("wbc", [P, D])
        put, cur = overlay(late + 8 * KB)
        u2 = put("u2", [P, NT, D])
        bank = [ctx.enter_context(nc.psum_tensor(f"bank{i}", [P, TN], F32)) for i in range(8)]

        sems = {}

        def S(name):
            if name not in sems:
                sems[name] = ctx.enter_context(nc.semaphore(name))
            return sems[name]

        block = ctx.enter_context(nc.Block())
        NPAIR = NE // 2

        def w_slice(name, row, col, width=TN):
            return A[name][0][row:row + TK * P, col:col + width].rearrange("(k p) n -> p k n", p=P)

        w_gu = A["w_gu"][0].rearrange("e (k p) n -> e p k n", p=P)
        w_dn = A["w_dn"][0].rearrange("e (k p) n -> e p k n", p=P)
        MOE_COLS = {"G0": (w_gu, 0), "G1": (w_gu, TN), "U0": (w_gu, D), "U1": (w_gu, D + TN),
                    "D0": (w_dn, 0), "D1": (w_dn, TN)}
        BIAS_COLS = {"G0": 0, "G1": TN, "U0": D, "U1": D + TN, "D0": 2 * D, "D1": 2 * D + TN}
        POSTS = {}
        for n, blk in enumerate(BLOCKS):
            POSTS[LAST_TILE[blk[:2]]] = (n, blk)
        CONV_TILE = {"x": 0, "B": DI // P, "C": DI // P + SG}
        OPERAND = {"kvdt": xta, "q": xta, "B": xta, "C": xta, "x": xta, "z": xta, "gate": xta, "so": xts,
                   "ao": xtb, "ck": xtm, "cv": xtm, "o": xtb, "cq": xta, "co": xtb}
        FM_KINDS = ("q", "B", "C", "x", "z", "ck", "cq")
        OPERAND_FROM = {"kvdt": "u_rows", "ck": "mem_rows", "o": "merged_made", "cq": "hn_rows", "co": "cross"}
        CROSS_ORDER = [("cs", 0), ("cs", 1)]
        for hh in range(CH):
            CROSS_ORDER += [("ct", hh)] + ([("cs", hh + 2)] if hh + 2 < CH else []) + [("cp", hh)]
        SLOPE = [2.0 ** (-8.0 * (i + 1) / HQ) for i in range(HQ)]

        class Uses:

            def __init__(self, eng):
                self.eng, self.n = eng, [0] * 8

            def claim(self, b):
                if self.n[b]:
                    self.eng.wait_ge(S(f"bank{b}_free"), self.n[b])

            def full(self, b):
                self.eng.wait_ge(S(f"bank{b}_full"), self.n[b] + 1)

            def next(self, *banks):
                for b in banks:
                    self.n[b] += 1

        def wait_read(eng, kind, arg):
            n = POSTS[LAST_TILE[kind, arg]][0]
            eng.wait_ge(S(f"pair{n % 2}_free"), n // 2 + 1)

        moe_base = [0] * RAW_MOE
        for t in range(TD):
            moe_base[t % RAW] += 32 if t <= LAST_TILE["kvdt", 0] else 16

        def wait_products(eng, it, p, j):
            if p.is_split[j]:
                eng.wait_ge(S("pe_tiles"), it * NSPLIT + (TD + PRO + p.splits_before(j) + 1))
            else:
                eng.wait_ge(S("pe_direct"), it * NDIRECT + (j - p.splits_before(j) + 1))

        def wait_parts(eng, it, p, j):
            if p.by_pool[j]:
                eng.wait_ge(S("lo_by_pool"), it * NPOOL + (p.pool_before(j) + 1))
            else:
                eng.wait_ge(S("lo_done"), it * (NSPLIT - NPOOL) +
                            (TD + PRO + p.splits_before(j) - p.pool_before(j) + 1))

        def has_low(kind):
            return any((kind, half) not in DIRECT for half in range(2))

        NLOW = sum(has_low(kind) for kind, _ in EVERY.blocks)

        def low_count(it, p, b):
            return it * NLOW + (2 + sum(has_low(kind) for kind, _ in p.blocks[:b + 1]))

        def chain_of(eng, sem):
            class Chain:
                count, base = 0, 0

                def done(self, ins):
                    ins.then_inc(S(sem), 1)
                    self.count += 1
                    return self.count

                def wait(self, upto=None):
                    eng.wait_ge(S(sem), self.base + (self.count if upto is None else upto))
            return Chain()

        @block.sync
        def _(sp):
            xv = A["x"][0].rearrange("(c p) d -> p c d", p=P)
            for c in range(NT):
                sp.dma_start(h[:, c, :], xv[:, c, :]).then_inc(S("x_loaded"), 16)
            sp.dma_start(vecs[:, :], A["vecs"]).then_inc(S("vecs_loaded"), 16)
            sp.dma_start(rows[:, :], A["rows"].to_broadcast([P, NR])).then_inc(S("rows_loaded"), 16)
            t = 0
            for kind, _, w, row, col, tiles in BLOCKS:
                for i in range(tiles):
                    dst = raw[t % RAW]
                    if t >= RAW:
                        sp.wait_ge(S("lo_done"), t - RAW + 1)
                    loaded = S(f"raw{t % RAW}_loaded")
                    if kind == "kvdt":
                        r = TK * P * i
                        sp.dma_start(dst[:, :, 0:2 * KVD], w_slice(w, r, C_K, 2 * KVD)).then_inc(loaded, 16)
                        sp.dma_start(dst[:, :, 2 * KVD:2 * KVD + SH], w_slice(w, r, C_DT, SH)).then_inc(loaded, 16)
                    else:
                        sp.dma_start(dst[:, :, :], w_slice(w, row + TK * P * i, col)).then_inc(loaded, 16)
                    t += 1

            def moe_load(m, kind, expert, half):
                src, col = MOE_COLS[kind]
                ap = src[expert, :, TK * half:TK * half + TK, col:col + TN]
                return sp.dma_start(raw_moe[m % RAW_MOE][:, :, :], ap)

            pro = [(k, 0, half) for k in ("G0", "U0") for half in range(2)]
            first = pro + EVERY.tiles
            for m in range(RAW_MOE):
                if m < RAW:
                    sp.wait_ge(S("lo_done"), 1 + max(t for t in range(TD) if t % RAW == m))
                elif m == RAW:
                    sp.wait_ge(S("pe_tiles"), LAST_TILE["co", 1] + 1)
                kind, a, half = first[m]
                moe_load(m, kind, a, half).then_inc(S(f"raw{m % RAW_MOE}_loaded"), 16)
            for m in range(PRO):
                sp.wait_ge(S("lo_done"), TD + m + 1)
                kind, a, half = first[m + RAW_MOE]
                moe_load(m, kind, a, half).then_inc(S(f"raw{m}_loaded"), 16)
            sp.wait_ge(S("rounds_made"), 1)
            end = sp.value_load(last_pass[0:1, 0:1], min_val=NPAIR - 1, max_val=NPAIR * ROUNDS - 1)

            def refill(it, experts, p, j):
                ahead = p.tiles + EVERY.tiles
                kind, a, half = ahead[j + RAW_MOE]
                a += 2 * ((j + RAW_MOE) // len(p.tiles))
                slot = (PRO + j) % RAW_MOE
                if p.is_split[j]:
                    wait_parts(sp, it, p, j)
                else:
                    wait_products(sp, it, p, j)
                moe_load(slot, kind, experts[a], half).then_inc(S(f"raw{slot}_loaded"), 16)

            def experts_of(it):
                return [sp.snap(sp.to_reg((it * 2 + a) & (NE - 1)), min_val=0, max_val=NE - 1) for a in range(4)]

            with sp.Fori(0, end) as it:
                experts = experts_of(it)
                for j in range(NTILE):
                    refill(it, experts, EVERY, j)
            experts = experts_of(end)
            for j in range(len(LAST.tiles) - RAW_MOE):
                refill(end, experts, LAST, j)
            sp.wait_ge(S("gathered"), end * 2 + 2)
            sp.dma_start(fw[:, :], A["final_norm_w"].to_broadcast([P, D])).then_inc(S("fw_loaded"), 16)
            for c in range(NT):
                sp.wait_ge(S("out_rows"), c + 1)
                sp.dma_start(out[0, c * P:(c + 1) * P, :], h[:, c, :]).then_inc(S("stored"), 16)
            sp.wait_ge(S("stored"), 16 * NT)

        @block.tensor
        def _(pe):
            mm, tr = nc.tensor.matmul, nc.tensor.transpose
            use = Uses(pe)
            free_pair = [0, 0]

            moved = {}

            def wait_moved(*key):
                for b, count in moved[key if len(key) > 1 else key[0]]:
                    pe.wait_ge(S(f"bank{b}_free"), count)

            def passes(outp, pairs, first, last):
                res = None
                for n, (s_hi, s_lo, m_hi, m_lo, kind) in enumerate(pairs):
                    trio = [(s_hi, m_hi), (s_hi, m_lo) if kind == "FM" else (s_lo, m_hi),
                            (s_lo, m_hi) if kind == "FM" else (s_hi, m_lo)]
                    for j, (a, b) in enumerate(trio):
                        res = mm(outp, a, b, start=first and n == 0 and j == 0,
                                 stop=last and n == len(pairs) - 1 and j == 2, skip_group_check=True)
                return res

            def rows_to_features(src, ready, count, banks=(4, 5, 6, 7)):
                pe.wait_ge(S(ready), count)
                for b2 in range(KD // 2):
                    b = banks[b2 % len(banks)]
                    use.claim(b)
                    for k in range(2):
                        for c in range(NT):
                            f = (2 * b2 + k) * P
                            res = tr(bank[b][:, k * T + c * P:k * T + (c + 1) * P], src[:, c, f:f + P], ident[:, :])
                    res.then_inc(S(f"bank{b}_full"), 1)
                    use.next(b)
                moved[ready] = [(b, use.n[b]) for b in banks]

            def stage(what, arg):
                if what == "decay":
                    pe.wait_ge(S("a_made"), 1)
                    use.claim(4)
                    for c in range(NT):
                        mm(bank[4][:, c * SH:(c + 1) * SH], upto[:, :], a_t[:, c, :], start=c == 0, stop=True,
                           skip_group_check=True)
                    mm(bank[4][:, NT * SH:(NT + 1) * SH], ones[:, :], a_t[:, 0, :], start=False, stop=True,
                       skip_group_check=True).then_inc(S("bank4_full"), 1)
                    use.next(4)
                elif what == "scores":
                    hp, = arg
                    g = hp // (HQ // 2 // HKV)
                    if hp == 0:
                        wait_moved("kvdt")
                    wait_read(pe, "q", hp // TK)
                    use.claim(4)
                    mm(bank[4][:, :], qt[:, hp, P:T], kpad[:, g, :, :], start=True, stop=True
                       ).then_inc(S("bank4_full"), 1)
                    use.claim(5)
                    mm(bank[5][:, 0:T], qt[:, hp, 0:P], kpad[:, g, :, 0:P], start=True, stop=True
                       ).then_inc(S("bank5_full"), 1)
                    use.next(4, 5)
                elif what == "pt":
                    hp, = arg
                    pe.wait_ge(S("probs_made"), hp + 1)
                    use.claim(6)
                    for hd in range(2):
                        for kc in range(2):
                            res = tr(bank[6][:, (2 * hd + kc) * P:(2 * hd + kc + 1) * P],
                                     sc[hp % 2][:, hd, kc * P:(kc + 1) * P], ident[:, :])
                    res.then_inc(S("bank6_full"), 1)
                    use.claim(5)
                    for hd in range(2):
                        res = tr(bank[5][:, T + hd * P:T + (hd + 1) * P], sc[hp % 2][:, hd, T:T + P], ident[:, :])
                    res.then_inc(S("bank5_full"), 1)
                    use.next(5, 6)
                    moved["pt", hp] = [(5, use.n[5]), (6, use.n[6])]
                elif what == "pv":
                    hp, = arg
                    g = hp // (HQ // 2 // HKV)
                    wait_moved("pt", hp)
                    use.claim(7)
                    o = bank[7][:, :].rearrange("p (h t) -> p h t", h=2)
                    mm(o[:, :, P:T], v2[:, 0, g, :], pt[:, :, 0, :], start=True, stop=False, skip_group_check=True)
                    mm(o[:, :, P:T], v2[:, 1, g, :], pt[:, :, 1, :], start=False, stop=True, skip_group_check=True)
                    mm(o[:, :, 0:P], v2[:, 0, g, :], pt[:, :, 2, :], start=False, stop=True, skip_group_check=True
                       ).then_inc(S("bank7_full"), 1)
                    use.next(7)
                    moved["pv", hp] = [(7, use.n[7])]
                elif what == "cb":
                    pe.wait_ge(S("bc_made"), 2)
                    for c in range(NT):
                        use.claim(4 + c)
                        for g in range(SG):
                            res = mm(bank[4 + c][:, g * P:(g + 1) * P], bt[:, g, c * P:(c + 1) * P],
                                     ct[:, g, c * P:(c + 1) * P], start=g == 0, stop=True, skip_group_check=True)
                        res.then_inc(S(f"bank{4 + c}_full"), 1)
                    use.claim(6)
                    for g in range(SG):
                        res = tr(bank[6][:, g * P:(g + 1) * P], bt[:, g, 0:P], ident[:, :])
                    res.then_inc(S("bank6_full"), 1)
                    use.next(4, 5, 6)
                    moved["cb", 0] = [(4, use.n[4]), (5, use.n[5]), (6, use.n[6])]
                elif what == "xt":
                    g, = arg
                    pe.wait_ge(S("xconv_made"), g + 1)
                    for c in range(NT):
                        use.claim(4 + c)
                        for m in range(TK):
                            res = tr(bank[4 + c][:, m * P:(m + 1) * P], xt[g % 2][:, m, c * P:(c + 1) * P], ident[:, :])
                        res.then_inc(S(f"bank{4 + c}_full"), 1)
                    use.next(4, 5)
                    moved["xt", g] = [(4, use.n[4]), (5, use.n[5])]
                elif what == "state":
                    g, = arg
                    if g == 0:
                        wait_moved("cb", 0)
                    wait_moved("xt", g)
                    use.claim(5)
                    mm(bank[5][:, :], btok[:, g, :], xdd[:, :], start=True, stop=True).then_inc(S("bank5_full"), 1)
                    use.next(5)
                    moved["state", g] = [(5, use.n[5])]
                elif what == "decays":
                    g, q = arg
                    c, half = divmod(q, 2)
                    use.claim(4)
                    for i in range(4):
                        head = GH * g + 4 * half + i
                        res = mm(bank[4][:, i * P:(i + 1) * P], a_t[:, c, head:head + 1].to_broadcast([P, P]),
                                 upto[:, :], start=i == 0, stop=True, skip_group_check=True)
                    res.then_inc(S("bank4_full"), 1)
                    use.next(4)
                elif what == "y":
                    g, q = arg
                    c, half = divmod(q, 2)
                    b = 6 + c
                    pe.wait_ge(S("gm_made"), 4 * g + q + 1)
                    if c == 1 and half == 0:
                        wait_moved("state", g)
                    if q == 0:
                        wait_moved("xt", g)
                    if half == 0 and g:
                        pe.wait_ge(S("y_read"), 2 * g - 1 + c)
                    elif half == 0:
                        use.claim(b)
                    for i in range(4):
                        head = 4 * half + i
                        o = bank[b][64 * (head % 2):64 * (head % 2) + 64, (head // 2) * P:(head // 2 + 1) * P]
                        first = half == 0 and i < 2
                        res = mm(o, xdt[:, c, head * 64:head * 64 + 64], gm[q % 2][:, i, :], start=first,
                                 stop=c == 0, skip_group_check=True)
                        if c == 1:
                            res = mm(o, h0[:, head * 64:head * 64 + 64], cte[q % 2][:, i, :], start=False,
                                     stop=True, skip_group_check=True)
                    res.then_inc(S("y_made"), 1)
                elif what == "norm":
                    g, = arg
                    pe.wait_ge(S("ysq_made"), g + 1)
                    use.claim(5)
                    for m in range(TK):
                        res = mm(bank[5][:, 0:T], ones[:, :], ysq[:, m, :], start=m == 0, stop=m == TK - 1)
                    res.then_inc(S("bank5_full"), 1)
                    use.next(5)
                elif what == "merged":
                    rows_to_features(att, "merged_made", 1)
                elif what == "mem":
                    pe.wait_ge(S("y_read"), 2 * SG)
                    rows_to_features(memx, "mem_rows", 1)
                elif what == "cross_in":
                    rows_to_features(xs, "hn_rows", 1)
                elif what == "cross":
                    for step, hh in CROSS_ORDER:
                        if step == "cs":
                            b = 4 + hh % 2
                            if hh == 0:
                                for half in range(2):
                                    wait_read(pe, "cq", half)
                                    wait_read(pe, "cv", half)
                                    wait_read(pe, "ck", half)
                            use.claim(b)
                            for c in range(NT):
                                for k in range(2):
                                    res = mm(bank[b][:, c * T:(c + 1) * T], cqt[:, 2 * hh + k, c * P:(c + 1) * P],
                                             ckt[:, 2 * hh + k, :], start=c == 0 and k == 0, stop=k == 1,
                                             skip_group_check=True)
                            res.then_inc(S(f"bank{b}_full"), 1)
                            use.next(b)
                        elif step == "ct":
                            pe.wait_ge(S("cprobs_made"), hh + 1)
                            use.claim(6)
                            for mc in range(2):
                                for c in range(NT):
                                    res = tr(bank[6][:, mc * T + c * P:mc * T + (c + 1) * P],
                                             csc[hh % 2][:, c, mc * P:(mc + 1) * P], ident[:, :])
                            res.then_inc(S("bank6_full"), 1)
                            use.next(6)
                            moved["cpt", hh] = [(6, use.n[6])]
                        else:
                            wait_moved("cpt", hh)
                            use.claim(7)
                            for dd in range(2):
                                for mc in range(2):
                                    f = hh * CHD + dd * P
                                    res = mm(bank[7][:, dd * T:(dd + 1) * T], cv[:, mc, f:f + P],
                                             cpt[hh % 2][:, mc, :], start=dd == 0 and mc == 0, stop=mc == 1,
                                             skip_group_check=True)
                            res.then_inc(S("bank7_full"), 1)
                            use.next(7)
                            moved["cross"] = [(7, use.n[7])]
                elif what == "router":
                    rows_to_features(u2, "u2_made", 1)
                    wait_moved("u2_made")
                    pe.wait_ge(S("wr_loaded"), 16)
                    use.claim(4)
                    for c in range(NT):
                        for k in range(KD):
                            res = mm(bank[4][:, c * NE:(c + 1) * NE], u2t[:, k, c * P:(c + 1) * P], w_r[:, k, :],
                                     start=c == 0 and k == 0, stop=k == KD - 1, skip_group_check=True)
                    res.then_inc(S("bank4_full"), 1)
                    use.next(4)
                    pe.wait_ge(S("mask_made"), 1)
                    use.claim(5)
                    mm(bank[5][:, 0:NE], before[:, :], mask[:, 0, :], start=True, stop=True, skip_group_check=True)
                    mm(bank[5][:, NE:2 * NE], ones[:, :], mask[:, 0, :], start=False, stop=False, skip_group_check=True)
                    mm(bank[5][:, NE:2 * NE], before[:, :], mask[:, 1, :], start=False, stop=True, skip_group_check=True)
                    mm(bank[5][:, 2 * NE:3 * NE], ones[:, :], mask[:, 0, :], start=False, stop=False,
                       skip_group_check=True)
                    mm(bank[5][:, 2 * NE:3 * NE], ones[:, :], mask[:, 1, :], start=False, stop=True,
                       skip_group_check=True).then_inc(S("bank5_full"), 1)
                    use.next(5)

            pe.wait_ge(S("consts_made"), 1)
            rows_to_features(memx, "u_rows", 1)
            t = 0
            for n, (kind, arg, w, row, col, tiles) in enumerate(BLOCKS):
                x, pair = OPERAND[kind], n % 2
                if n >= 2:
                    pe.wait_ge(S(f"pair{pair}_free"), n // 2)
                if kind == "so":
                    pe.wait_ge(S("ssm_lo"), arg[0] + 1)
                elif kind == "ao":
                    for hp in range(HQ // 2):
                        wait_moved("pv", hp)
                elif kind in OPERAND_FROM:
                    wait_moved(OPERAND_FROM[kind])
                for i in range(tiles):
                    pe.wait_ge(S("lo_done"), t + 1)
                    hi, lo = w_hi[t % HL], w_lo[t % HL]
                    first, last = i == 0, i == tiles - 1
                    if kind == "kvdt":
                        width = 2 * KVD + SH
                        use.claim(4)
                        res = passes(bank[4][:, 0:T], [(hi[:, kk, 0:KVD], lo[:, kk, 0:KVD], x[:, 0, TK * i + kk, :],
                                                        x[:, 1, TK * i + kk, :], "FM") for kk in range(TK)], first, last)
                        if last:
                            res.then_inc(S("bank4_full"), 1)
                            use.next(4)
                            moved["kvdt"] = [(4, use.n[4])]
                    else:
                        width = TN
                    if kind in FM_KINDS:
                        for m in range(TK):
                            o = bank[2 * pair + m // 2][:, (m % 2) * T:(m % 2 + 1) * T]
                            res = passes(o, [(hi[:, kk, m * P:(m + 1) * P], lo[:, kk, m * P:(m + 1) * P],
                                              x[:, 0, TK * i + kk, :], x[:, 1, TK * i + kk, :], "FM")
                                             for kk in range(TK)], first and m % 2 == 0, last)
                    else:
                        for c in range(NT):
                            cs = slice(c * P, (c + 1) * P)
                            res = passes(bank[2 * pair + c][:, 0:width],
                                         [(x[:, 0, TK * i + kk, cs], x[:, 1, TK * i + kk, cs], hi[:, kk, 0:width],
                                           lo[:, kk, 0:width], "TM") for kk in range(TK)], first, last)
                    res.then_inc(S("pe_tiles"), 1)
                    for what, *rest in stages_after(t):
                        stage(what, rest)
                    t += 1

            def split_tile(acc, lhs, kk0, slot, last):
                for kk in range(TK):
                    st = lhs[:, kk0 + kk, :]
                    mm(bank[acc][:, :], st, hi_moe[slot][:, kk, :], start=False, stop=False, skip_group_check=True)
                    res = mm(bank[acc][:, :], st, lo_moe[slot][:, kk, :], start=False, stop=last and kk == TK - 1,
                             skip_group_check=True)
                res.then_inc(S("pe_tiles"), 1)

            def bias_row(acc, kind, par, picked):
                pe.wait_ge(S("bias_picked"), picked)
                mm(bank[acc][:, :], bsel[par][:, :], btab[:, BIAS_COLS[kind]:BIAS_COLS[kind] + TN],
                   start=True, stop=False, skip_group_check=True)

            def block_products(it, p, b, acc):
                kind, a = p.blocks[b]
                bias_row(acc, kind, a % 2, it * 2 + (a + 1))
                lhs = ae[a % 2] if kind[0] == "D" else xe[a % 2]
                for half in range(2):
                    j = 2 * b + half
                    if p.is_split[j]:
                        k = p.splits_before(j)
                        wait_parts(pe, it, p, j)
                        split_tile(acc, lhs, TK * half, (PRO + k) % HL_MOE, half == 1)
                    else:
                        m = PRO + j
                        slot = m % RAW_MOE
                        pe.wait_ge(S(f"raw{slot}_loaded"), it * (16 * NTILE // RAW_MOE) +
                                   (moe_base[slot] + 16 * (m // RAW_MOE + 1)))
                        pe.wait_ge(S("af_made"), it * 2 + (a + 1))
                        for kk in range(TK):
                            res = mm(bank[acc][0:SLOTS, :], af[:, TK * half + kk, :], raw_moe[slot][:, kk, :],
                                     start=False, stop=half == 1 and kk == TK - 1, skip_group_check=True)
                        res.then_inc(S("pe_direct"), 1)

            def gather(par, e_count):
                pe.wait_ge(S("sel_made"), e_count * 2)
                if not isinstance(e_count, int) or e_count > 1:
                    pe.wait_ge(S("xe_made"), e_count - 1)
                for k in range(KD):
                    for j in range(3):
                        for c in range(NT):
                            res = mm(bank[4][:, k * SLOTS:(k + 1) * SLOTS], xp[j][:, c, k * P:(k + 1) * P],
                                     sel[par][:, c, :], start=k == 0 and j == 0 and c == 0,
                                     stop=j == 2 and c == 1, skip_group_check=True)
                res.then_inc(S("gathered"), 1)

            def act_transposes(made, free_sem, free_count):
                pe.wait_ge(S("act_made"), made)
                if free_sem:
                    pe.wait_ge(S(free_sem), free_count)
                for k in range(TK):
                    res = tr(bank[5][:, k * P:(k + 1) * P], aa[:, k * P:(k + 1) * P], ident[:, :])
                res.then_inc(S("bank5_moe"), 1)

            pe.wait_ge(S("moe_ready"), 1)
            end = pe.value_load(last_pass[0:1, 0:1], min_val=NPAIR - 1, max_val=NPAIR * ROUNDS - 1)
            gather(0, 1)
            pe.wait_ge(S("xe_made"), 1)
            for acc, kind in ((2, "G0"), (3, "U0")):
                bias_row(acc, kind, 0, 1)
                for half in range(2):
                    m = 2 * (acc - 2) + half
                    pe.wait_ge(S("lo_done"), TD + m + 1)
                    split_tile(acc, xe[0], TK * half, m % HL_MOE, half == 1)
            act_transposes(1, None, 0)

            def combine(it, c, folds):
                if c == 0:
                    pe.wait_ge(S("folded"), folds)
                    pe.wait_ge(S("back_made"), it + 1)
                for half in range(2):
                    pe.wait_ge(S(f"bank{6 + half}_added"), it * 2 + (c + 1))
                    mm(bank[6 + half][:, :], back[:, c * P:(c + 1) * P], oex[:, half * TN:(half + 1) * TN],
                       start=True, stop=True).then_inc(S("combined"), 1)

            def body(it, last):
                p = LAST if last else EVERY
                for b, (kind, a) in enumerate(p.blocks):
                    if kind == "G1" and not (last and a == 1):
                        gather((a + 1) % 2, it * 2 + (a + 2))
                    if kind == "G0":
                        pe.wait_ge(S("xe_made"), it * 2 + (a + 1))
                    if kind == "D0":
                        pe.wait_ge(S("ae_made"), it * 4 + (2 * a + 2))
                    pe.wait_ge(S("folded"), it * NB + (b + 1))
                    block_products(it, p, b, b % 4)
                    if a == 0 and kind in ("G1", "U1"):
                        combine(it, 0 if kind == "G1" else 1, it * NB + 4)
                    if kind == "G0" or (kind == "U1" and last and a == 1):
                        ea_ = a - 1 if kind == "G0" else a
                        k = 2 if ea_ == 0 else 4
                        act_transposes(it * 4 + k, "ae_made", it * 4 + (k - 1))
                    if (kind == "U0" and a == 2) or (kind == "U1" and last and a == 1):
                        pe.wait_ge(S("selg_made"), it * 2 + 2)
                        pe.wait_ge(S("ae_made"), it * 4 + 4)
                        for c in range(NT):
                            res = tr(bank[5][:, c * P:(c + 1) * P], selg[:, c, :], ident[:, :])
                        res.then_inc(S("bank5_moe"), 1)
                    if kind == "D0" and not (last and a == 1):
                        if a == 0:
                            act_transposes(it * 4 + 3, "ae_made", it * 4 + 2)
                        else:
                            act_transposes(it * 4 + 5, "back_made", it + 2)

            with pe.Fori(0, end) as it:
                body(it, False)
            body(end, True)
            for c in range(NT):
                combine(end + 1, c, end * NB + (NB + 2))

        @block.scalar
        def _(act):
            A_ = nc.scalar.activation
            use = Uses(act)

            def high_part(t, src, hi, wait_slot, loaded, loaded_count):
                act.wait_ge(S(loaded), loaded_count)
                if wait_slot is not None:
                    act.wait_ge(S("pe_tiles"), wait_slot)
                return A_(hi, src, ACT.Copy)

            loaded = [0] * RAW

            def split_dense(t):
                if t >= TD:
                    return
                kind = next(b[0] for b in BLOCKS if LAST_TILE[b[:2]] >= t)
                loaded[t % RAW] += 32 if kind == "kvdt" else 16
                width = 2 * KVD + SH if kind == "kvdt" else TN
                high_part(t, raw[t % RAW][:, :, 0:width], w_hi[t % HL][:, :, 0:width],
                          t - HL + 1 if t >= HL else None, f"raw{t % RAW}_loaded", loaded[t % RAW]
                          ).then_inc(S("hi_done"), 1)

            def norm_rows(src, dst, name, cols):
                for c in range(NT):
                    res = A_(dst[:, c, :], src[:, c, :], ACT.Square, accum_out=stat[:, cols + c:cols + c + 1])
                res.then_inc(S(name + "_ms"), 1)
                act.wait_ge(S(name + "_var"), 1)
                A_(stat[:, cols + 2:cols + 4], stat[:, cols + 2:cols + 4], ACT.Sqrt).then_inc(S(name + "_sd"), 1)

            def features_hi(dst, name, scale_col):
                for b2 in range(KD // 2):
                    b = 4 + b2
                    use.full(b)
                    for k in range(2):
                        src = bank[b][:, k * T:(k + 1) * T]
                        if scale_col is None:
                            res = A_(dst[:, 0, 2 * b2 + k, :], src, ACT.Copy)
                        else:
                            c = scale_col + 2 * b2 + k
                            res = A_(dst[:, 0, 2 * b2 + k, :], src, ACT.Identity, scale=vecs[:, c:c + 1])
                    res.then_inc(S(name), 1)
                    use.next(b)

            def stage(what, arg):
                if what == "decay":
                    act.wait_ge(S("dt_abs"), 1)
                    A_(tmp32[:, 1, :], tmp32[:, 1, :], ACT.Exp).then_inc(S("dt_exp"), 1)
                    act.wait_ge(S("rows_loaded"), 16)
                    A_(tmp32[:, 5, 0:SH], rows[:, R_ALOG:R_ALOG + SH], ACT.Exp).then_inc(S("dt_exp"), 1)
                    act.wait_ge(S("dt_one"), 1)
                    A_(tmp32[:, 3, :], tmp32[:, 2, :], ACT.Ln).then_inc(S("dt_ln"), 1)
                    act.wait_ge(S("bank4_free"), use.n[4] + 1)
                    A_(ddt[:, :], ddt[:, :], ACT.Exp).then_inc(S("decay_made"), 1)
                    use.next(4)
                elif what == "scores":
                    hp, = arg
                    par = hp % 2
                    act.wait_ge(S("max_made"), hp + 1)
                    m = 16 * par
                    for hd in range(2):
                        for c, cols in ((1, slice(0, T)), (0, slice(T, T + P))):
                            i = m + 2 * c + hd
                            A_(sc[par][:, hd, cols], sc[par][:, hd, cols], ACT.Exp, bias=stat[:, i:i + 1],
                               accum_out=stat[:, i + 4:i + 5]).then_inc(S("exps_made"), 1)
                    A_(stat[:, m + 8:m + 12], stat[:, m + 8:m + 12], ACT.Exp).then_inc(S("exps_made"), 1)
                    use.next(4, 5)
                elif what == "pt":
                    hp, = arg
                    use.full(6)
                    A_(pt[:, :, 0:2, :], bank[6][:, :].rearrange("p (h k t) -> p h k t", h=2, k=2), ACT.Copy
                       ).then_inc(S("bank6_free"), 1)
                    use.full(5)
                    A_(pt[:, :, 2, :], bank[5][:, T:2 * T].rearrange("p (h t) -> p h t", h=2), ACT.Copy
                       ).then_inc(S("bank5_free"), 1)
                    use.next(5, 6)
                elif what == "pv":
                    hp, = arg
                    use.full(7)
                    for hd in range(2):
                        r = slice(64 * hd, 64 * hd + 64)
                        res = A_(xtb[r, 0, hp, :], bank[7][r, hd * T:(hd + 1) * T], ACT.Copy)
                    res.then_inc(S("attn_hi"), 1)
                    use.next(7)
                elif what == "cb":
                    use.full(6)
                    A_(btok[:, :, :], bank[6][:, :].rearrange("p (g n) -> p g n", g=SG), ACT.Copy
                       ).then_inc(S("bank6_free"), 1)
                    use.next(4, 5, 6)
                elif what == "xt":
                    use.next(4, 5)
                elif what == "state":
                    g, = arg
                    use.full(5)
                    if g:
                        act.wait_ge(S("y_made"), 4 * g)
                    A_(h0[:, :], bank[5][:, :], ACT.Copy).then_inc(S("bank5_free"), 1)
                    use.next(5)
                elif what == "decays":
                    g, q = arg
                    c = q // 2
                    par = q % 2
                    if c == 1:
                        use.full(4)
                        if 4 * g + q > 2:
                            act.wait_ge(S("cte_made"), 2 * g + q - 2)
                        A_(ea[:, :, :], bank[4][:, :].rearrange("p (i l) -> p i l", i=4), ACT.Exp
                           ).then_inc(S("ea_made"), 1)
                    act.wait_ge(S("bank4_free"), use.n[4] + 1)
                    A_(seg[par][:, :, :], seg[par][:, :, :], ACT.Exp).then_inc(S("lmat_made"), 1)
                    use.next(4)
                elif what == "y":
                    g, q = arg
                    if q == 3:
                        act.wait_ge(S("yz_made"), g + 1)
                        if g:
                            act.wait_ge(S("yvar_made"), g)
                        A_(ysq[:, :, :], yt[:, :, :], ACT.Square).then_inc(S("ysq_made"), 1)
                elif what == "norm":
                    g, = arg
                    act.wait_ge(S("yvar_made"), g + 1)
                    A_(rs[:, :], rs[:, :], ACT.Sqrt).then_inc(S("ysd_made"), 1)
                    act.wait_ge(S("yn_made"), g + 1)
                    if g:
                        act.wait_ge(S("pe_tiles"), LAST_TILE["so", (g - 1, 1)] + 1)
                    for m in range(TK):
                        c = V_SSMW + TK * g + m
                        res = A_(xts[:, 0, m, :], yt[:, m, :], ACT.Identity, scale=vecs[:, c:c + 1])
                    res.then_inc(S("ssm_hi"), 1)
                    use.next(5)
                elif what == "merged":
                    features_hi(xtb, "merged_hi", None)
                elif what == "mem":
                    act.wait_ge(S("mem_loaded"), 16)
                    norm_rows(memx, cv, "mem", 32)
                    features_hi(xtm, "mem_hi", V_MEM)
                elif what == "cross_in":
                    for half in range(2):
                        wait_read(act, "o", half)
                    norm_rows(h, xs, "hn", 36)
                    features_hi(xta, "hn_hi", V_CROSS)
                elif what == "cross":
                    for step, hh in CROSS_ORDER:
                        par = hh % 2
                        if step == "cs":
                            act.wait_ge(S("cmax_made"), hh + 1)
                            for c in range(NT):
                                i = 4 * par + c
                                A_(csc[par][:, c, :], csc[par][:, c, :], ACT.Exp, bias=stat[:, i:i + 1],
                                   accum_out=stat[:, i + 2:i + 3]).then_inc(S("cexp_made"), 1)
                            use.next(4 + par)
                        elif step == "ct":
                            use.full(6)
                            A_(cpt[par][:, :, :], bank[6][:, :].rearrange("p (m t) -> p m t", m=2), ACT.Copy
                               ).then_inc(S("bank6_free"), 1)
                            use.next(6)
                        else:
                            use.full(7)
                            A_(xtb[:, 0, 2 * hh:2 * hh + 2, :], bank[7][:, :].rearrange("p (d t) -> p d t", d=2),
                               ACT.Copy).then_inc(S("cross_hi"), 1)
                            use.next(7)
                elif what == "router":
                    for half in range(2):
                        wait_read(act, "co", half)
                    norm_rows(h, u2, "ffn", 40)
                    for b2 in range(KD // 2):
                        use.full(4 + b2)
                        A_(u2t[:, 2 * b2:2 * b2 + 2, :], bank[4 + b2][:, :].rearrange("p (k t) -> p k t", k=2),
                           ACT.Copy).then_inc(S(f"bank{4 + b2}_free"), 1)
                        use.next(4 + b2)
                    act.wait_ge(S("u2_made"), 1)
                    A_(xp[0][:, :, :], u2[:, :, :], ACT.Copy).then_inc(S("part0_made"), 1)
                    use.next(4)
                    act.wait_ge(S("top_made"), 1)
                    for c in range(NT):
                        A_(top8[:, c, 0:TOPK], top8[:, c, 0:TOPK], ACT.Exp, bias=stat[:, 44 + c:45 + c],
                           accum_out=stat[:, 46 + c:47 + c]).then_inc(S("top_exp"), 1)
                    act.wait_ge(S("rest1_made"), 1)
                    A_(xp[1][:, :, :], u2[:, :, :], ACT.Copy).then_inc(S("part1_made"), 1)
                    use.next(5)

            act.wait_ge(S("x_loaded"), 16 * NT)
            norm_rows(h, memx, "u", 48)
            split_dense(0)
            act.wait_ge(S("vecs_loaded"), 16)
            features_hi(xta, "u_hi", V_MIX)
            split_dense(1)
            silu_next = None
            for t in range(TD):
                split_dense(t + HL)
                act.wait_ge(S("pe_tiles"), t + 1)
                if silu_next is not None:
                    kind, arg, dst = silu_next
                    wait_read(act, kind, arg)
                    if kind == "x" and arg >= 2:
                        act.wait_ge(S("y_read"), 2 * (arg - 1))
                    A_(dst[:, :, :], conv[:, :, :], ACT.Silu).then_inc(
                        S("xconv_made" if kind == "x" else "bc_made"), 1)
                    silu_next = None
                if t in POSTS:
                    nb, (kind, arg, *_) = POSTS[t]
                    pb = 2 * (nb % 2)
                    pair = [bank[pb + i][:, :].rearrange("p (m t) -> p m t", m=2) for i in range(2)]
                    freed = S(f"pair{nb % 2}_free")
                    if kind == "kvdt":
                        use.next(4)
                    elif kind == "q":
                        for i in range(2):
                            res = A_(qt[:, TK * arg + 2 * i:TK * arg + 2 * i + 2, :], pair[i], ACT.Copy, scale=HD ** -0.5)
                        res.then_inc(freed, 1)
                    elif kind in CONV_TILE:
                        ct0 = CONV_TILE[kind] + (TK * arg if kind == "x" else 0)
                        for m in range(TK):
                            w3 = V_CONVW + 4 * (ct0 + m) + 3
                            b = V_CONVB + ct0 + m
                            res = A_(conv[:, m, :], pair[m // 2][:, m % 2, :], ACT.Identity, bias=vecs[:, b:b + 1],
                                     scale=vecs[:, w3:w3 + 1])
                        res.then_inc(S("conv_first"), 1)
                        silu_next = (kind, arg, {"x": xt[arg % 2], "B": bt, "C": ct}[kind])
                    elif kind == "z":
                        if arg >= 2:
                            act.wait_ge(S("yz_made"), arg - 1)
                        for i in range(2):
                            res = A_(zt[arg % 2][:, 2 * i:2 * i + 2, :], pair[i], ACT.Silu)
                        res.then_inc(freed, 1)
                    elif kind == "so" and arg[0] == 0:
                        for c in range(NT):
                            res = A_(ssm[:, c, TN * arg[1]:TN * arg[1] + TN], bank[pb + c][:, :], ACT.Copy)
                        res.then_inc(freed, 1)
                    elif kind == "ao":
                        for c in range(NT):
                            res = A_(att[:, c, TN * arg:TN * arg + TN], bank[pb + c][:, :], ACT.Copy)
                        res.then_inc(freed, 1)
                    elif kind == "gate":
                        act.wait_ge(S("gate_sum"), 2 * arg[0] + arg[1] + 1)
                        A_(sig[:, :, :], sig[:, :, :], ACT.Sigmoid).then_inc(S("gate_sig"), 1)
                    elif kind == "ck":
                        for i in range(2):
                            res = A_(ckt[:, TK * arg + 2 * i:TK * arg + 2 * i + 2, :], pair[i], ACT.Copy)
                        res.then_inc(freed, 1)
                    elif kind == "cv":
                        for c in range(NT):
                            res = A_(cv[:, c, TN * arg:TN * arg + TN], bank[pb + c][:, :], ACT.Copy)
                        res.then_inc(freed, 1)
                    elif kind == "cq":
                        for i in range(2):
                            res = A_(cqt[:, TK * arg + 2 * i:TK * arg + 2 * i + 2, :], pair[i], ACT.Copy,
                                     scale=CHD ** -0.5)
                        res.then_inc(freed, 1)
                for what, *rest in stages_after(t):
                    stage(what, rest)

            def split_moe(split_no, slot, m, loaded_count):
                raw_slot = m % RAW_MOE
                act.wait_ge(S(f"raw{raw_slot}_loaded"), loaded_count)
                act.wait_ge(S("pe_tiles"), split_no - HL_MOE + 1)
                A_(hi_moe[slot][:, :, :], raw_moe[raw_slot][:, :, :], ACT.Copy).then_inc(S("hi_done"), 1)

            def split_of_pass(it, p, k):
                m = PRO + (p.splits + [NTILE + j for j in EVERY.splits])[k]
                split_moe(it * NSPLIT + (TD + PRO + k), (PRO + k) % HL_MOE, m, it * (16 * NTILE // RAW_MOE) +
                          (moe_base[m % RAW_MOE] + 16 * (m // RAW_MOE + 1)))

            act.wait_ge(S("rounds_made"), 1)
            end = act.value_load(last_pass[0:1, 0:1], min_val=NPAIR - 1, max_val=NPAIR * ROUNDS - 1)

            def move_low(acc, count):
                act.wait_ge(S("folded"), count)
                A_(low, bank[acc][SLOTS:P, :], ACT.Copy).then_inc(S("low_made"), 1)

            def silu_gate(count):
                act.wait_ge(S("gate_clamped"), count)
                A_(gs[:, :], gg, ACT.Silu, scale=ALPHA).then_inc(S("gate_silu"), 1)

            def gathered_hi(par, count):
                act.wait_ge(S("gathered"), count)
                A_(xe[par][:, :, 0:SLOTS], bank[4][:, :].rearrange("p (k s) -> p k s", s=SLOTS), ACT.Copy
                   ).then_inc(S("xe_hi"), 1)

            def acts_hi(par, half, count):
                act.wait_ge(S("bank5_moe"), count)
                A_(ae[par][:, TK * half:TK * half + TK, 0:SLOTS],
                   bank[5][:, :].rearrange("p (k s) -> p k s", s=P)[:, :, 0:SLOTS], ACT.Copy, scale=1.0 / ALPHA
                   ).then_inc(S("ae_hi"), 1)

            assert PRO == HL_MOE
            for m in range(HL_MOE):
                if m == HL:
                    act.wait_ge(S("pe_tiles"), TD)
                    act.wait_ge(S("bias_split"), 3)
                split_moe(TD + m, m, m, moe_base[m] + 16)
                if m == 1:
                    gathered_hi(0, 1)
            for m in range(PRO):
                split_of_pass(0, EVERY, m)
                if m == 1:
                    move_low(2, 2)
                elif m == 3:
                    move_low(3, 3)
                    silu_gate(1)
            acts_hi(0, 0, 1)

            def split_after(it, p, j):
                k = p.splits_before(j) + HL_MOE
                if p.is_split[j] and not (p is LAST and k >= len(p.splits)):
                    split_of_pass(it, p, k)

            def body(it, last):
                p = LAST if last else EVERY
                for b, (kind, a) in enumerate(p.blocks):
                    split_after(it, p, 2 * b)
                    if kind == "G1" and not (last and a == 1):
                        gathered_hi((a + 1) % 2, it * 2 + (a + 2))
                    if has_low(kind):
                        wait_products(act, it, p, 2 * b + 1)
                        move_low(b % 4, it * NB + (b + 3 + 1))
                    if kind[0] == "U":
                        silu_gate(it * 4 + {("U1", 0): 2, ("U0", 1): 3, ("U1", 1): 4, ("U0", 2): 5}[kind, a])
                    if kind == "G0":
                        acts_hi((a - 1) % 2, 1, it * 5 + (2 if a == 1 else 4))
                    if kind == "U1" and last and a == 1:
                        acts_hi(1, 1, it * 5 + 4)
                    if kind == "D0" and not (last and a == 1):
                        acts_hi((a + 1) % 2, 0, it * 5 + (3 if a == 0 else 6))
                    split_after(it, p, 2 * b + 1)

            with act.Fori(0, end) as it:
                body(it, False)
            body(end, True)
            act.wait_ge(S("tokens_done"), 1)
            for c in range(NT):
                res = A_(raw_moe[RAW][:, 2 * c:2 * c + 2, :].rearrange("p k n -> p (k n)"), h[:, c, :], ACT.Square, accum_out=stat[:, 52 + c:53 + c])
            res.then_inc(S("out_ms"), 1)
            act.wait_ge(S("out_var"), 1)
            A_(stat[:, 54:56], stat[:, 54:56], ACT.Sqrt).then_inc(S("out_sd"), 1)

        @block.vector
        def _(dve):
            V = nc.vector
            use = Uses(dve)
            ch = chain_of(dve, "dve_own")
            CHAIN_PER_PASS = 0

            def split_dense(t):
                if t >= TD:
                    return
                kind = next(b[0] for b in BLOCKS if LAST_TILE[b[:2]] >= t)
                width = 2 * KVD + SH if kind == "kvdt" else TN
                dve.wait_ge(S("hi_done"), t + 1)
                V.tensor_tensor(w_lo[t % HL][:, :, 0:width], raw[t % RAW][:, :, 0:width],
                                w_hi[t % HL][:, :, 0:width].bitcast(F32), ALU.subtract).then_inc(S("lo_done"), 1)

            def norm_rows(src, dst, name, cols, made, weight=None):
                dve.wait_ge(S(name + "_ms"), 1)
                V.tensor_scalar(stat[:, cols + 2:cols + 4], stat[:, cols:cols + 2], 1.0 / D, EPS, ALU.mult, ALU.add
                                ).then_inc(S(name + "_var"), 1)
                dve.wait_ge(S(name + "_sd"), 1)
                ch.done(V.reciprocal(stat[:, cols:cols + 2], stat[:, cols + 2:cols + 4]))
                ch.wait()
                for c in range(NT):
                    if weight is None:
                        res = V.tensor_scalar(dst[:, c, :], src[:, c, :], stat[:, cols + c:cols + c + 1], None, ALU.mult)
                    else:
                        res = V.scalar_tensor_tensor(dst[:, c, :], src[:, c, :], stat[:, cols + c:cols + c + 1],
                                                     weight, ALU.mult, ALU.mult)
                res.then_inc(S(made), 1)

            def features_lo(dst, hi_name, scale_col):
                for b2 in range(KD // 2):
                    b = 4 + b2
                    dve.wait_ge(S(hi_name), b2 + 1)
                    for k in range(2):
                        src = bank[b][:, k * T:(k + 1) * T]
                        hi = dst[:, 0, 2 * b2 + k, :].bitcast(F32)
                        if scale_col is None:
                            res = V.tensor_tensor(dst[:, 1, 2 * b2 + k, :], src, hi, ALU.subtract)
                        else:
                            c = scale_col + 2 * b2 + k
                            res = V.scalar_tensor_tensor(dst[:, 1, 2 * b2 + k, :], src, vecs[:, c:c + 1], hi,
                                                         ALU.mult, ALU.subtract)
                    res.then_inc(S(f"bank{b}_free"), 1)
                    use.next(b)

            def stage(what, arg):
                if what == "decay":
                    both = lambda i: tmp32[:, i, :]
                    ch.done(V.scalar_tensor_tensor(both(1), both(0), -1.0, both(0), ALU.mult, ALU.min))
                    ch.wait()
                    V.tensor_scalar(both(0), both(0), 0.0, None, ALU.max).then_inc(S("dt_abs"), 1)
                    dve.wait_ge(S("dt_exp"), 1)
                    V.tensor_scalar(both(2), both(1), 1.0, None, ALU.add).then_inc(S("dt_one"), 1)
                    dve.wait_ge(S("dt_one"), 1)
                    ch.done(V.scalar_tensor_tensor(both(4), both(2), -1.0, both(1), ALU.add, ALU.subtract))
                    ch.wait()
                    ch.done(V.reciprocal(both(1), both(2)))
                    ch.wait()
                    ch.done(V.tensor_tensor(both(4), both(4), both(1), ALU.mult))
                    dve.wait_ge(S("dt_ln"), 1)
                    ch.done(V.tensor_tensor(both(0), both(0), both(3), ALU.add))
                    ch.wait()
                    ch.done(V.tensor_tensor(dts[:, :, :], both(0).rearrange("p (c h) -> p c h", c=NT),
                                            both(4).rearrange("p (c h) -> p c h", c=NT), ALU.subtract))
                    ch.wait()
                    dve.wait_ge(S("dt_exp"), 2)
                    for c in range(NT):
                        res = V.scalar_tensor_tensor(a_t[:, c, :], dts[:, c, :], -1.0, tmp32[:, 5, 0:SH],
                                                     ALU.mult, ALU.mult)
                    res.then_inc(S("a_made"), 1)
                    use.full(4)
                    ch.done(V.tensor_copy(acum[:, :, :], bank[4][:, 0:NT * SH].rearrange("p (c h) -> p c h", c=NT)))
                    ch.wait()
                    V.tensor_tensor(ddt[:, :], bank[4][:, NT * SH:(NT + 1) * SH], acum[:, 0, :], ALU.subtract
                                    ).then_inc(S("bank4_free"), 1)
                    use.next(4)
                    dve.wait_ge(S("decay_made"), 1)
                    ch.done(V.tensor_tensor(ddt[:, :], ddt[:, :], dts[:, 0, :], ALU.mult))
                elif what == "scores":
                    hp, = arg
                    par = hp % 2
                    m = 16 * par
                    if hp >= 2:
                        dve.wait_ge(S("bank5_full"), pt_full[hp - 2])
                    use.full(4)
                    use.full(5)
                    for hd in range(2):
                        head = 2 * hp + hd
                        ch.done(V.scalar_tensor_tensor(sc[par][:, hd, 0:T], dist[:, :], SLOPE[head],
                                                       bank[4][:, hd * T:(hd + 1) * T], ALU.mult, ALU.add)) \
                            if hd == 0 else \
                            V.scalar_tensor_tensor(sc[par][:, hd, 0:T], dist[:, :], SLOPE[head],
                                                   bank[4][:, hd * T:(hd + 1) * T], ALU.mult, ALU.add
                                                   ).then_inc(S("bank4_free"), 1)
                    for hd in range(2):
                        head = 2 * hp + hd
                        res = V.scalar_tensor_tensor(sc[par][:, hd, T:T + P], dist[:, P:2 * P], SLOPE[head],
                                                     bank[5][:, hd * P:(hd + 1) * P], ALU.mult, ALU.add)
                        if hd == 0:
                            ch.done(res)
                    res.then_inc(S("bank5_free"), 1)
                    use.next(4, 5)
                    dve.wait_ge(S("bank4_free"), use.n[4])
                    dve.wait_ge(S("bank5_free"), use.n[5])
                    ch.wait()
                    ch.done(V.reduce_max(stat[:, m + 2:m + 4], sc[par][:, :, 0:T], AX))
                    ch.done(V.reduce_max(stat[:, m:m + 2], sc[par][:, :, T:T + P], AX))
                    ch.wait()
                    sink = rows[:, R_SINK + 2 * hp:R_SINK + 2 * hp + 2]
                    for c in range(NT):
                        i = m + 2 * c
                        ch.done(V.tensor_tensor(stat[:, i:i + 2], stat[:, i:i + 2], sink, ALU.max))
                    ch.wait()
                    for c in range(NT):
                        i = m + 2 * c
                        ch.done(V.tensor_tensor(stat[:, i + 8:i + 10], sink, stat[:, i:i + 2], ALU.subtract))
                    ch.wait()
                    V.tensor_scalar(stat[:, m:m + 4], stat[:, m:m + 4], -1.0, None, ALU.mult).then_inc(S("max_made"), 1)
                elif what == "probs":
                    hp, = arg
                    par = hp % 2
                    m = 16 * par
                    dve.wait_ge(S("exps_made"), 5 * (hp + 1))
                    ch.done(V.tensor_tensor(stat[:, m + 4:m + 8], stat[:, m + 4:m + 8], stat[:, m + 8:m + 12], ALU.add))
                    ch.wait()
                    ch.done(V.reciprocal(stat[:, m + 12:m + 16], stat[:, m + 4:m + 8]))
                    ch.wait()
                    for hd in range(2):
                        for c, cols in ((1, slice(0, T)), (0, slice(T, T + P))):
                            i = m + 12 + 2 * c + hd
                            res = V.tensor_scalar(sc[par][:, hd, cols], sc[par][:, hd, cols], stat[:, i:i + 1],
                                                  None, ALU.mult)
                    res.then_inc(S("probs_made"), 1)
                elif what == "pt":
                    hp, = arg
                    use.next(5, 6)
                    pt_full[hp] = use.n[5]
                elif what == "pv":
                    hp, = arg
                    dve.wait_ge(S("attn_hi"), hp + 1)
                    for hd in range(2):
                        r = slice(64 * hd, 64 * hd + 64)
                        res = V.tensor_tensor(xtb[r, 1, hp, :], bank[7][r, hd * T:(hd + 1) * T],
                                              xtb[r, 0, hp, :].bitcast(F32), ALU.subtract)
                    res.then_inc(S("bank7_free"), 1)
                    use.next(7)
                elif what == "cb":
                    for c in range(NT):
                        use.full(4 + c)
                        V.tensor_tensor(cbt[:, c, :, :], bank[4 + c][:, :].rearrange("p (g l) -> p g l", g=SG),
                                        upto[:, :].rearrange("p (o l) -> p o l", o=1).to_broadcast([P, SG, P]),
                                        ALU.mult).then_inc(S(f"bank{4 + c}_free"), 1)
                    use.next(4, 5, 6)
                    cb_uses.extend([(4, use.n[4]), (5, use.n[5])])
                elif what == "xt":
                    g, = arg
                    if g:
                        dve.wait_ge(S("y_made"), 4 * g)
                    ch.wait()
                    for c in range(NT):
                        use.full(4 + c)
                    scale = lambda ap: ap.rearrange("p (h o) -> p h o", o=1).to_broadcast([P, GH, 64])
                    x3 = lambda ap: ap.rearrange("p (h q) -> p h q", h=GH)
                    hs = slice(GH * g, GH * g + GH)
                    ch.done(V.tensor_tensor(x3(xdt[:, 0, :]), x3(bank[4][:, :]), scale(dts[:, 0, hs]), ALU.mult))
                    V.tensor_tensor(x3(xdd[:, :]), x3(bank[4][:, :]), scale(ddt[:, hs]), ALU.mult
                                    ).then_inc(S("bank4_free"), 1)
                    V.tensor_tensor(x3(xdt[:, 1, :]), x3(bank[5][:, :]), scale(dts[:, 1, hs]), ALU.mult
                                    ).then_inc(S("bank5_free"), 1)
                    use.next(4, 5)
                elif what == "state":
                    use.next(5)
                elif what == "decays":
                    g, q = arg
                    c, half = divmod(q, 2)
                    par = q % 2
                    if g == 0 and q == 0:
                        for b, count in cb_uses:
                            dve.wait_ge(S(f"bank{b}_free"), count)
                    use.full(4)
                    if c == 1:
                        dve.wait_ge(S("ea_made"), 2 * g + half + 1)
                    n_y = 4 * g + q - 2 + 1
                    if n_y > 0:
                        dve.wait_ge(S("lmat_made"), n_y)
                    for i in range(4):
                        head = GH * g + 4 * half + i
                        res = V.tensor_scalar(seg[par][:, i, :], bank[4][:, i * P:(i + 1) * P],
                                              acum[:, c, head:head + 1], 0.0, ALU.subtract, ALU.min)
                    res.then_inc(S("bank4_free"), 1)
                    dve.wait_ge(S("lmat_made"), 4 * g + q + 1)
                    if n_y > 0:
                        dve.wait_ge(S("y_made"), n_y)
                    grp = cbt[:, c, g:g + 1, :].to_broadcast([P, 4, P])
                    if c == 1:
                        V.tensor_tensor(cte[par][:, :, :], ct[:, g:g + 1, P:T].to_broadcast([P, 4, P]), ea[:, :, :],
                                        ALU.mult).then_inc(S("cte_made"), 1)
                    V.tensor_tensor(gm[par][:, :, :], seg[par][:, :, :], grp, ALU.mult).then_inc(S("gm_made"), 1)
                    use.next(4)
                elif what == "y":
                    g, q = arg
                    if q % 2 == 1:
                        c = q // 2
                        b = 6 + c
                        dve.wait_ge(S("y_made"), 4 * g + q + 1)
                        if g:
                            dve.wait_ge(S("ssm_lo"), g)
                        for m in range(TK):
                            col = V_SKIP + TK * g + m
                            res = V.scalar_tensor_tensor(yt[:, m, c * P:(c + 1) * P], xt[g % 2][:, m, c * P:(c + 1) * P],
                                                         vecs[:, col:col + 1], bank[b][:, m * P:(m + 1) * P],
                                                         ALU.mult, ALU.add)
                            if m < 3:
                                ch.done(res)
                        res.then_inc(S("y_read"), 1)
                elif what == "norm":
                    g, = arg
                    use.full(5)
                    V.tensor_scalar(rs[:, :], bank[5][:, 0:T], 1.0 / TN, EPS, ALU.mult, ALU.add
                                    ).then_inc(S("yvar_made"), 1)
                    dve.wait_ge(S("ysd_made"), g + 1)
                    V.reciprocal(rs[:, :], rs[:, :]).then_inc(S("bank5_free"), 1)
                    use.next(5)
                    dve.wait_ge(S("bank5_free"), use.n[5])
                    V.tensor_tensor(yt[:, :, :], yt[:, :, :],
                                    rs[:, :].rearrange("p (o t) -> p o t", o=1).to_broadcast([P, TK, T]), ALU.mult
                                    ).then_inc(S("yn_made"), 1)
                    dve.wait_ge(S("ssm_hi"), g + 1)
                    for m in range(TK):
                        col = V_SSMW + TK * g + m
                        res = V.scalar_tensor_tensor(xts[:, 1, m, :], yt[:, m, :], vecs[:, col:col + 1],
                                                     xts[:, 0, m, :].bitcast(F32), ALU.mult, ALU.subtract)
                        if m < 3:
                            ch.done(res)
                    res.then_inc(S("ssm_lo"), 1)
                elif what == "merged":
                    features_lo(xtb, "merged_hi", None)
                elif what == "mem":
                    norm_rows(memx, memx, "mem", 32, "mem_rows")
                    features_lo(xtm, "mem_hi", V_MEM)
                elif what == "cross_in":
                    norm_rows(h, xs, "hn", 36, "hn_rows")
                    features_lo(xta, "hn_hi", V_CROSS)
                elif what == "cross":
                    for step, hh in CROSS_ORDER:
                        par = hh % 2
                        if step == "cs":
                            use.full(4 + par)
                            if hh >= 2:
                                dve.wait_ge(S("bank6_full"), cross_full[hh - 2])
                            V.tensor_copy(csc[par][:, :, :], bank[4 + par][:, :].rearrange("p (c m) -> p c m", c=NT)
                                          ).then_inc(S(f"bank{4 + par}_free"), 1)
                            use.next(4 + par)
                            dve.wait_ge(S(f"bank{4 + par}_free"), use.n[4 + par])
                            ch.done(V.reduce_max(stat[:, 4 * par:4 * par + 2], csc[par][:, :, :], AX))
                            ch.wait()
                            V.tensor_scalar(stat[:, 4 * par:4 * par + 2], stat[:, 4 * par:4 * par + 2], -1.0, None,
                                            ALU.mult).then_inc(S("cmax_made"), 1)
                            dve.wait_ge(S("cexp_made"), 2 * (hh + 1))
                            ch.done(V.reciprocal(stat[:, 8 + 2 * par:10 + 2 * par], stat[:, 4 * par + 2:4 * par + 4]))
                            ch.wait()
                            for c in range(NT):
                                res = V.tensor_scalar(csc[par][:, c, :], csc[par][:, c, :],
                                                      stat[:, 8 + 2 * par + c:9 + 2 * par + c], None, ALU.mult)
                                if c == 0:
                                    ch.done(res)
                            res.then_inc(S("cprobs_made"), 1)
                        elif step == "ct":
                            use.next(6)
                            cross_full[hh] = use.n[6]
                        else:
                            dve.wait_ge(S("cross_hi"), hh + 1)
                            V.tensor_tensor(xtb[:, 1, 2 * hh:2 * hh + 2, :],
                                            bank[7][:, :].rearrange("p (d t) -> p d t", d=2),
                                            xtb[:, 0, 2 * hh:2 * hh + 2, :].bitcast(F32), ALU.subtract
                                            ).then_inc(S("bank7_free"), 1)
                            use.next(7)
                elif what == "router":
                    dve.wait_ge(S("wffn_loaded"), 16)
                    norm_rows(h, u2, "ffn", 40, "u2_made", weight=wbc[:, :])
                    for b in range(4, 8):
                        use.next(b)
                    use.full(4)
                    br = rows[:, R_BR:R_BR + NE].rearrange("p (o e) -> p o e", o=1).to_broadcast([P, NT, NE])
                    V.tensor_tensor(logit[:, :, :], bank[4][:, 0:NT * NE].rearrange("p (c e) -> p c e", c=NT), br,
                                    ALU.add).then_inc(S("logits_made"), 1)
                    use.next(4)
                    dve.wait_ge(S("logits_made"), 1)
                    for c in range(NT):
                        ch.done(V.max(top8[:, c, :], logit[:, c, :]))
                    ch.wait()
                    for c in range(NT):
                        ch.done(V.max_index(idx8[:, c, :], top8[:, c, :], logit[:, c, :]))
                    ch.wait()
                    ch.done(V.tensor_copy(idxf[:, :, :], idx8[:, :, :]))
                    V.tensor_scalar(stat[:, 44:46], top8[:, :, 0:1].rearrange("p c o -> p (c o)"), -1.0, None, ALU.mult
                                    ).then_inc(S("top_made"), 1)
                    ch.wait()
                    for c in range(NT):
                        for j in range(TOPK):
                            if j == 0:
                                ch.done(V.tensor_scalar(mask[:, c, :], iota[:, 0:NE], idxf[:, c, 0:1], None, ALU.is_equal))
                                ch.wait()
                            else:
                                res = V.scalar_tensor_tensor(mask[:, c, :], iota[:, 0:NE], idxf[:, c, j:j + 1],
                                                             mask[:, c, :], ALU.is_equal, ALU.add)
                                if c == NT - 1 and j == TOPK - 1:
                                    res.then_inc(S("mask_made"), 1)
                                else:
                                    ch.done(res)
                                    ch.wait()
                    dve.wait_ge(S("top_exp"), NT)
                    ch.done(V.reciprocal(stat[:, 48:50], stat[:, 46:48]))
                    ch.wait()
                    for c in range(NT):
                        ch.done(V.tensor_scalar(top8[:, c, 0:TOPK], top8[:, c, 0:TOPK], stat[:, 48 + c:49 + c], None,
                                                ALU.mult))
                    ch.wait()
                    for c in range(NT):
                        for j in range(TOPK):
                            w = top8[:, c, j:j + 1]
                            if j == 0:
                                ch.done(V.tensor_scalar(gate[:, c, :], iota[:, 0:NE], idxf[:, c, 0:1], w,
                                                        ALU.is_equal, ALU.mult))
                                ch.wait()
                            else:
                                ch.done(V.tensor_scalar(eq[:, :], iota[:, 0:NE], idxf[:, c, j:j + 1], w,
                                                        ALU.is_equal, ALU.mult))
                                ch.wait()
                                ch.done(V.tensor_tensor(gate[:, c, :], gate[:, c, :], eq[:, :], ALU.add))
                                ch.wait()
                    for r in range(ROUNDS):
                        ch.done(V.tensor_copy(gate4[:, :, r * NE:(r + 1) * NE], gate[:, :, :]))
                    use.full(5)
                    place_ = bank[5][:, 0:2 * NE].rearrange("p (c e) -> p c e", c=NT)
                    ch.done(V.scalar_tensor_tensor(logit[:, :, :], place_, 4096.0, mask[:, :, :], ALU.add, ALU.mult))
                    ch.done(V.reduce_max(stat[:, 56:57], bank[5][:, 2 * NE:3 * NE], AX))
                    ch.wait()
                    for r in range(ROUNDS):
                        ch.done(V.tensor_scalar(pos4[:, :, r * NE:(r + 1) * NE], logit[:, :, :],
                                                -4096.0 - SLOTS * r, None, ALU.add))
                    for r in range(1, ROUNDS):
                        ch.done(V.tensor_scalar(stat[:, 56 + r:57 + r], stat[:, 56:57], float(SLOTS * r), float(NPAIR),
                                                ALU.is_gt, ALU.mult))
                    ch.wait()
                    ch.done(V.tensor_scalar(stat[:, 60:61], stat[:, 57:58], float(NPAIR - 1), stat[:, 58:59], ALU.add, ALU.add))
                    ch.wait()
                    V.tensor_tensor(last_pass[:, :], stat[:, 60:61], stat[:, 59:60], ALU.add).then_inc(S("rounds_made"), 1)
                    use.next(5)
                    dve.wait_ge(S("part0_made"), 1)
                    V.tensor_tensor(u2[:, :, :], u2[:, :, :], xp[0][:, :, :], ALU.subtract).then_inc(S("rest1_made"), 1)
                    dve.wait_ge(S("part1_made"), 1)
                    ch.done(V.tensor_tensor(u2[:, :, :], u2[:, :, :], xp[1][:, :, :], ALU.subtract))
                    ch.wait()
                    V.tensor_copy(xp[2][:, :, :], u2[:, :, :]).then_inc(S("parts_made"), 1)

            pt_full, cross_full, cb_uses, marks = {}, {}, [], [0] * TK
            dve.wait_ge(S("consts_made"), 1)
            norm_rows(h, memx, "u", 48, "u_rows")
            split_dense(0)
            dve.wait_ge(S("vecs_loaded"), 16)
            features_lo(xta, "u_hi", V_MIX)
            split_dense(1)
            conv_no = 0
            for t in range(TD):
                split_dense(t + HL)
                dve.wait_ge(S("pe_tiles"), t + 1)
                if t in POSTS:
                    nb, (kind, arg, *_) = POSTS[t]
                    pb = 2 * (nb % 2)
                    freed = S(f"pair{nb % 2}_free")
                    if kind == "kvdt":
                        for c in range(NT):
                            ch.done(V.tensor_copy(
                                v2[:, c, :, :].rearrange("p g (o d) -> p g o d", o=2),
                                bank[pb + c][:, KVD:2 * KVD].rearrange("p (g o d) -> p g o d", g=HKV, o=1)
                                .to_broadcast([P, HKV, 2, HD])))
                        dve.wait_ge(S("rows_loaded"), 16)
                        for c in range(NT):
                            res = V.tensor_tensor(tmp32[:, 0, c * SH:(c + 1) * SH], bank[pb + c][:, 2 * KVD:2 * KVD + SH],
                                                  rows[:, R_DTB:R_DTB + SH], ALU.add)
                            if c == 0:
                                ch.done(res)
                        res.then_inc(freed, 1)
                        dve.wait_ge(freed, nb // 2 + 1)
                        use.full(4)
                        lo_, hi_ = slice(0, 64), slice(64, P)
                        for g, src in ((0, lo_), (1, hi_)):
                            for odd, dst in ((0, lo_), (1, hi_)):
                                res = V.tensor_copy(kpad[dst, g, odd, :], bank[4][src, 0:T])
                                if not (g and odd):
                                    ch.done(res)
                        res.then_inc(S("bank4_free"), 1)
                        use.next(4)
                    elif kind in CONV_TILE:
                        ct0 = CONV_TILE[kind] + (TK * arg if kind == "x" else 0)
                        conv_no += 1
                        dve.wait_ge(S("conv_first"), conv_no)
                        for tap in range(2, -1, -1):
                            back_ = 3 - tap
                            for m in range(TK):
                                src = bank[pb + m // 2][:, (m % 2) * T:(m % 2) * T + T - back_]
                                w = V_CONVW + 4 * (ct0 + m) + tap
                                if tap < 2:
                                    ch.wait(marks[m])
                                res = V.scalar_tensor_tensor(conv[:, m, back_:], src, vecs[:, w:w + 1],
                                                             conv[:, m, back_:], ALU.mult, ALU.add)
                                if tap or m < TK - 1:
                                    mark = ch.done(res)
                                    marks[m] = mark
                        res.then_inc(freed, 1)
                    elif kind == "so" and arg[0] > 0:
                        for c in range(NT):
                            cols = slice(TN * arg[1], TN * arg[1] + TN)
                            if arg[0] == 1:
                                wait_read(dve, "so", (0, arg[1]))
                            elif c == 0:
                                wait_read(dve, "so", (arg[0] - 1, arg[1]))
                            res = V.tensor_tensor(ssm[:, c, cols], bank[pb + c][:, :], ssm[:, c, cols], ALU.add)
                            if c == 0:
                                ch.done(res)
                        res.then_inc(freed, 1)
                    elif kind == "gate":
                        b, n = arg
                        order = 2 * b + n + 1
                        cols = slice(TN * n, TN * n + TN)
                        if order == 1:
                            dve.wait_ge(S("bgate_loaded"), 16)
                        else:
                            wait_read(dve, "gate", ((order - 2) // 2, (order - 2) % 2))
                        ch.wait()
                        for c in range(NT):
                            w = bgate[:, D * b + TN * n:D * b + TN * n + TN]
                            res = V.tensor_tensor(sig[:, c, :], bank[pb + c][:, :], w, ALU.add)
                            if c == 0:
                                ch.done(res)
                        res.then_inc(S("gate_sum"), 1)
                        dve.wait_ge(S("gate_sig"), order)
                        if b == 0:
                            wait_read(dve, "ao", n)
                            V.tensor_tensor(att[:, :, cols], att[:, :, cols], sig[:, :, :], ALU.mult).then_inc(freed, 1)
                        else:
                            wait_read(dve, "so", (SG - 1, n))
                            wait_read(dve, "gate", (0, n))
                            V.tensor_tensor(sig[:, :, :], ssm[:, :, cols], sig[:, :, :], ALU.mult).then_inc(freed, 1)
                            dve.wait_ge(freed, nb // 2 + 1)
                            res = V.tensor_tensor(att[:, :, cols], att[:, :, cols], sig[:, :, :], ALU.add)
                            if n == 0:
                                ch.done(res)
                            else:
                                res.then_inc(S("merged_made"), 1)
                    elif kind in ("o", "co"):
                        cols = slice(TN * arg, TN * arg + TN)
                        for c in range(NT):
                            res = V.tensor_tensor(h[:, c, cols], bank[pb + c][:, :], h[:, c, cols], ALU.add)
                            if c == 0:
                                ch.done(res)
                        res.then_inc(freed, 1)
                for what, *rest in stages_after(t):
                    stage(what, rest)

            for buf in (aa, oex, back):
                ch.done(V.memset(buf[:, :], 0.0))
            ch.wait()
            dve.wait_ge(S("parts_made"), 1)
            for i, sem in enumerate(("folded", "folded", "back_made", "bank6_added", "bank7_added", "moe_ready")):
                V.memset(eq[:, i:i + 1], 0.0).then_inc(S(sem), 1)
            dve.wait_ge(S("rounds_made"), 1)
            end = dve.value_load(last_pass[0:1, 0:1], min_val=NPAIR - 1, max_val=NPAIR * ROUNDS - 1)

            def split_moe(split_no, slot, m):
                dve.wait_ge(S("hi_done"), split_no + 1)
                V.tensor_tensor(lo_moe[slot][:, :, :], raw_moe[m % RAW_MOE][:, :, :], hi_moe[slot][:, :, :].bitcast(F32),
                                ALU.subtract).then_inc(S("lo_done"), 1)

            def split_of_pass(it, p, k):
                j = (p.splits + [NTILE + j for j in EVERY.splits])[k]
                if not (p.by_pool + EVERY.by_pool)[j]:
                    split_moe(it * NSPLIT + (TD + PRO + k), (PRO + k) % HL_MOE, PRO + j)

            def fold_gate(acc, block, lows):
                dve.wait_ge(S("low_made"), lows)
                V.tensor_tensor(gg, bank[acc][0:SLOTS, :], low, ALU.add).then_inc(S("folded"), 1)
                dve.wait_ge(S("folded"), block + 2)
                V.tensor_scalar(gg, gg, LIMIT, None, ALU.min).then_inc(S("gate_clamped"), 1)

            def fold_up(acc, block, lows, gates, transposed):
                dve.wait_ge(S("low_made"), lows)
                V.tensor_tensor(uu[:, :], bank[acc][0:SLOTS, :], low, ALU.add).then_inc(S("folded"), 1)
                dve.wait_ge(S("folded"), block + 2)
                V.tensor_scalar(uu[:, :], uu[:, :], LIMIT, -LIMIT, ALU.min, ALU.max).then_inc(S("up_clamped"), 1)
                dve.wait_ge(S("up_clamped"), gates)
                dve.wait_ge(S("gate_silu"), gates)
                if transposed is not None:
                    dve.wait_ge(S("bank5_moe"), transposed)
                V.scalar_tensor_tensor(aa[0:SLOTS, :], uu[:, :], 1.0, gs[:, :], ALU.add, ALU.mult
                                       ).then_inc(S("act_made"), 1)

            def gathered_lo(par, count):
                dve.wait_ge(S("xe_hi"), count)
                V.tensor_tensor(xe[par][:, :, SLOTS:P], bank[4][:, :].rearrange("p (k s) -> p k s", s=SLOTS),
                                xe[par][:, :, 0:SLOTS].bitcast(F32), ALU.subtract).then_inc(S("xe_made"), 1)

            def acts_lo(par, half, count):
                dve.wait_ge(S("ae_hi"), count)
                V.scalar_tensor_tensor(ae[par][:, TK * half:TK * half + TK, SLOTS:P],
                                       bank[5][:, :].rearrange("p (k s) -> p k s", s=P)[:, :, 0:SLOTS], 1.0 / ALPHA,
                                       ae[par][:, TK * half:TK * half + TK, 0:SLOTS].bitcast(F32), ALU.mult,
                                       ALU.subtract).then_inc(S("ae_made"), 1)

            def fold_out(acc, it, p, b):
                kind, a = p.blocks[b]
                n = int(kind[1])
                dst = oex[SLOTS * a:SLOTS * a + SLOTS, TN * n:TN * n + TN]
                if has_low(kind):
                    dve.wait_ge(S("low_made"), low_count(it, p, b))
                    res = V.tensor_tensor(dst, bank[acc][0:SLOTS, :], low, ALU.add)
                else:
                    wait_products(dve, it, p, 2 * b + 1)
                    res = V.tensor_copy(dst, bank[acc][0:SLOTS, :])
                res.then_inc(S("folded"), 1)

            def add_tokens(it, c):
                for half in range(2):
                    cols = slice(half * TN, (half + 1) * TN)
                    dve.wait_ge(S("combined"), it * 4 + (2 * c + half + 1))
                    dve.wait_ge(S(f"bank{6 + half}_added"), it * 2 + (c + 1))
                    V.tensor_tensor(h[:, c, cols], bank[6 + half][:, :], h[:, c, cols], ALU.add
                                    ).then_inc(S(f"bank{6 + half}_added"), 1)

            def select(par, idx, last_gated):
                if last_gated is not None:
                    dve.wait_ge(S("gathered"), last_gated)
                    dve.wait_ge(S("selg_made"), last_gated)
                for c in range(NT):
                    V.tensor_scalar(sel[par][:, c, :], iota[:, :], pos4[:, c, bass.ds(idx, 1)], None, ALU.is_equal
                                    ).then_inc(S("sel_made"), 1)

            select(0, 0, None)
            select(1, 1, None)
            for m in range(HL_MOE):
                split_moe(TD + m, m, m)
                if m == 1:
                    gathered_lo(0, 1)
            for m in range(PRO):
                split_of_pass(0, EVERY, m)
                if m == 1:
                    fold_gate(2, 1, 1)
                elif m == 3:
                    fold_up(3, 2, 2, 1, None)
            acts_lo(0, 0, 1)

            def split_after(it, p, j):
                k = p.splits_before(j) + HL_MOE
                if p.is_split[j] and not (p is LAST and k >= len(p.splits)):
                    split_of_pass(it, p, k)

            def body(it, last):
                p = LAST if last else EVERY
                for b, (kind, a) in enumerate(p.blocks):
                    if kind == "D0" and not last:
                        select(a, it * 2 + (a + 2), it * 2 + (a + 1))
                    split_after(it, p, 2 * b)
                    if kind == "G1" and not (last and a == 1):
                        gathered_lo((a + 1) % 2, it * 2 + (a + 2))
                    block_no = it * NB + (b + 3)
                    if kind[0] == "G":
                        fold_gate(b % 4, block_no, low_count(it, p, b))
                    elif kind[0] == "U":
                        k = {("U1", 0): 2, ("U0", 1): 3, ("U1", 1): 4, ("U0", 2): 5}[kind, a]
                        fold_up(b % 4, block_no, low_count(it, p, b), it * 4 + k, it * 5 + (k - 1))
                    else:
                        fold_out(b % 4, it, p, b)
                    if kind == "G0":
                        acts_lo((a - 1) % 2, 1, it * 4 + (2 if a == 1 else 4))
                    if kind == "U1" and last and a == 1:
                        acts_lo(1, 1, it * 4 + 4)
                    if kind == "D0" and not (last and a == 1):
                        acts_lo((a + 1) % 2, 0, it * 4 + (3 if a == 0 else 5))
                    split_after(it, p, 2 * b + 1)
                    if a == 0 and kind == "U1":
                        add_tokens(it, 0)
                    if a == 1 and kind == "G0":
                        add_tokens(it, 1)
                    if (kind == "U0" and a == 2) or (kind == "U1" and last and a == 1):
                        dve.wait_ge(S("bank5_moe"), it * 5 + 5)
                        dve.wait_ge(S("combined"), it * 4 + 4)
                        V.tensor_copy(back[:, :], bank[5][:, 0:T]).then_inc(S("back_made"), 1)

            with dve.Fori(0, end) as it:
                body(it, False)
            body(end, True)
            for c in range(NT):
                add_tokens(end + 1, c)
            for half in range(2):
                dve.wait_ge(S(f"bank{6 + half}_added"), end * 2 + 5)
            V.memset(eq[:, 0:1], 0.0).then_inc(S("tokens_done"), 1)
            dve.wait_ge(S("out_ms"), 1)
            V.tensor_scalar(stat[:, 54:56], stat[:, 52:54], 1.0 / D, EPS, ALU.mult, ALU.add).then_inc(S("out_var"), 1)
            dve.wait_ge(S("out_sd"), 1)
            V.reciprocal(stat[:, 52:54], stat[:, 54:56]).then_inc(S("out_rstd"), 1)
            dve.wait_ge(S("out_rstd"), 1)
            dve.wait_ge(S("fw_loaded"), 16)
            for c in range(NT):
                V.scalar_tensor_tensor(h[:, c, :], h[:, c, :], stat[:, 52 + c:53 + c], fw[:, :], ALU.mult, ALU.mult
                                       ).then_inc(S("out_rows"), 1)

        @block.gpsimd
        def _(pool):
            G = nc.gpsimd
            ch = chain_of(pool, "pool_own")
            pool.dma_start(w_r[:, :, :], A["w_router"][0].rearrange("(k p) e -> p k e", p=P)).then_inc(S("wr_loaded"), 16)
            for m, v in ((ident, 0.0), (upto, 1.0), (before, 1.0), (ones, 1.0)):
                ch.done(G.memset(m[:, :], v))
            ch.done(G.memset(pick[:, :], 0.0))
            ch.done(G.iota(iota[:, :], pattern=[[1, SLOTS]], base=0, channel_multiplier=0,
                           allow_small_or_imprecise_dtypes=True))
            ch.done(G.iota(dist[:, :], pattern=[[1, 2 * P]], base=-P, channel_multiplier=-1,
                           allow_small_or_imprecise_dtypes=True))
            ch.done(G.memset(kpad[:, :, :, :], 0.0))
            ch.wait()
            ch.done(G.affine_select(out=ident[:, :], in_=ident[:, :], compare_op=ALU.not_equal, fill=1.0, base=0,
                                    pattern=[[-1, P]], channel_multiplier=1))
            ch.done(G.affine_select(out=upto[:, :], in_=upto[:, :], compare_op=ALU.is_ge, fill=0.0, base=0,
                                    pattern=[[1, P]], channel_multiplier=-1))
            ch.done(G.affine_select(out=before[:, :], in_=before[:, :], compare_op=ALU.is_gt, fill=0.0, base=0,
                                    pattern=[[1, P]], channel_multiplier=-1))
            ch.done(G.affine_select(out=dist[:, :], in_=dist[:, :], compare_op=ALU.is_ge, fill=MASKED, base=P,
                                    pattern=[[-1, 2 * P]], channel_multiplier=1))
            ch.wait()
            ch.done(G.affine_select(out=dist[:, :], in_=dist[:, :], compare_op=ALU.is_gt, fill=MASKED, base=0,
                                    pattern=[[1, 2 * P]], channel_multiplier=-1))
            for k in range(2):
                ch.done(G.affine_select(out=pick[:, :], in_=pick[:, :], compare_op=ALU.not_equal, fill=1.0,
                                        base=-NE * k, pattern=[[0, ROUNDS], [-1, NE]], channel_multiplier=1))
                ch.wait()
            G.tensor_copy(cur_small[:, :], ident[:, 0:1]).then_inc(S("consts_made"), 1)

            for g in range(SG):
                pool.wait_ge(S("y_read"), 2 * (g + 1))
                wait_read(pool, "z", g)
                G.tensor_tensor(yt[:, :, :], yt[:, :, :], zt[g % 2][:, :, :], ALU.mult).then_inc(S("yz_made"), 1)
            pool.wait_ge(S("yz_made"), SG)
            pool.dma_start(bgate[:, :], A["b_gate"].to_broadcast([P, 2 * D])).then_inc(S("bgate_loaded"), 16)
            pool.dma_start(memx[:, :, :], A["mem"][0].rearrange("(c p) d -> p c d", p=P)).then_inc(S("mem_loaded"), 16)
            pool.wait_ge(S("merged_hi"), KD // 2)
            pool.wait_ge(S("merged_made"), 1)
            ch.done(G.memset(bst[:, :], 0.0))
            ch.wait()
            for r in range(2):
                rs_ = slice(NE * r, NE * (r + 1))
                pool.dma_start(bst[rs_, 0:2 * D], A["b_gu"][0]).then_inc(S("bias_loaded"), 16)
                pool.dma_start(bst[rs_, 2 * D:3 * D], A["b_dn"][0]).then_inc(S("bias_loaded"), 16)
            pool.wait_ge(S("pe_tiles"), LAST_TILE["co", 0])
            pool.dma_start(wbc[:, :], A["norm_ffn_w"].to_broadcast([P, D])).then_inc(S("wffn_loaded"), 16)
            pool.wait_ge(S("bias_loaded"), 64)
            G.tensor_copy(btab[:, :], bst[:, :]).then_inc(S("bias_split"), 1)
            pool.wait_ge(S("bias_split"), 1)
            low_rows = slice(NE, 2 * NE)
            G.tensor_tensor(bst[low_rows, :], bst[low_rows, :], btab[low_rows, :].bitcast(F32), ALU.subtract
                            ).then_inc(S("bias_split"), 1)
            pool.wait_ge(S("bias_split"), 2)
            G.tensor_copy(btab[low_rows, :], bst[low_rows, :]).then_inc(S("bias_split"), 1)
            pool.wait_ge(S("bias_split"), 3)
            for b in bsel:
                ch.done(G.memset(b[:, :].bitcast(F32), 0.0))
            ch.wait()

            pool.wait_ge(S("rounds_made"), 1)
            end = pool.value_load(last_pass[0:1, 0:1], min_val=NPAIR - 1, max_val=NPAIR * ROUNDS - 1)

            def pick_bias(par, idx):
                G.tensor_copy(bsel[par][:, 0:SLOTS], pick[:, bass.ds(idx, 1)].to_broadcast([P, SLOTS])
                              ).then_inc(S("bias_picked"), 1)

            pick_bias(0, 0)

            def split_of_pass(it, p, k):
                j = (p.splits + [NTILE + i for i in EVERY.splits])[k]
                if (p.by_pool + EVERY.by_pool)[j]:
                    slot = (PRO + k) % HL_MOE
                    pool.wait_ge(S("hi_done"), it * NSPLIT + (TD + PRO + k + 1))
                    G.tensor_tensor(lo_moe[slot][:, :, :], raw_moe[(PRO + j) % RAW_MOE][:, :, :],
                                    hi_moe[slot][:, :, :].bitcast(F32), ALU.subtract).then_inc(S("lo_by_pool"), 1)

            def split_after(it, p, j):
                k = p.splits_before(j) + HL_MOE
                if p.is_split[j] and not (p is LAST and k >= len(p.splits)):
                    split_of_pass(it, p, k)

            for k in range(PRO):
                split_of_pass(0, EVERY, k)

            def body(it, last):
                p = LAST if last else EVERY
                for b, (kind, a) in enumerate(p.blocks):
                    split_after(it, p, 2 * b)
                    if kind == "G1" and not (last and a == 1):
                        pool.wait_ge(S("gathered"), it * 2 + (a + 2))
                        pool.wait_ge(S("bias_picked"), it * 2 + (a + 1))
                        pick_bias((a + 1) % 2, it * 2 + (a + 1))
                    if kind == "G0" or (kind == "U1" and last and a == 1):
                        a_ = a - 1 if kind == "G0" else a
                        pool.wait_ge(S("ae_made"), it * 4 + (2 * a_ + 2))
                        G.tensor_tensor(af[:, :, :], ae[a_][:, :, 0:SLOTS].bitcast(F32),
                                        ae[a_][:, :, SLOTS:P].bitcast(F32), ALU.add).then_inc(S("af_made"), 1)
                        if a_ == 0:
                            pool.wait_ge(S("back_made"), it + 1)
                        else:
                            pool.wait_ge(S("selg_made"), it * 2 + 1)
                        pool.wait_ge(S("sel_made"), it * 4 + (2 * a_ + 2))
                        G.tensor_tensor(selg[:, :, SLOTS * a_:SLOTS * a_ + SLOTS], sel[a_][:, :, :],
                                        gate4[:, :, bass.ds(it * 2 + a_, 1)].to_broadcast([P, NT, SLOTS]), ALU.mult
                                        ).then_inc(S("selg_made"), 1)
                    split_after(it, p, 2 * b + 1)

            with pool.Fori(0, end) as it:
                body(it, False)
            body(end, True)


_INS = ["x", "mem", "vecs", "rows", "w_in", "w_gate", "b_gate", "w_attn_o", "w_ssm_o", "w_out", "w_cq", "w_ckv", "w_co",
        "norm_ffn_w", "w_router", "w_gu", "b_gu", "w_dn", "b_dn", "final_norm_w"]


def kernel(**inputs):
    import numpy as _np
    import concourse.bacc as _bacc
    from concourse import mybir as _mybir
    from concourse.bass_utils import run_bass_kernel_spmd as _run

    a = {k: _np.asarray(v) for k, v in inputs.items()}
    col = lambda v: v.reshape(-1, P).T
    conv = a["conv_w"][0].reshape(4, XBC // P, P).transpose(2, 1, 0).reshape(P, -1)
    skip = _np.broadcast_to(a["d_skip"][0][:, None], (SH, 64)).reshape(-1)
    a["vecs"] = _np.concatenate([col(a["norm_mix_w"][0]), col(a["norm_cross_w"][0]), col(a["norm_mem_w"][0]), conv,
                                 col(a["conv_b"][0]), col(a["ssm_norm_w"][0]), col(skip)], axis=1)
    a["rows"] = _np.concatenate([a["dt_bias"][0], a["a_log"][0], a["attn_sinks"][0], a["b_router"][0]])[None]
    a["final_norm_w"] = a["final_norm_w"][None]
    nc = _bacc.Bacc("TRN2", target_bir_lowering=False, num_devices=1)
    arrays, aps = {}, {}
    for name in _INS:
        v = _np.ascontiguousarray(a[name])
        arrays[f"in_{name}"] = v
        aps[name] = nc.dram_tensor(f"in_{name}", v.shape, _mybir.dt.from_np(v.dtype), kind="ExternalInput").ap()
    out = nc.dram_tensor("out", (1, T, D), _mybir.dt.float32, kind="ExternalOutput").ap()
    layer(nc, aps, out)
    r = _run(nc, [arrays], core_ids=[0])
    return r.results[0]["out"]
```
